# Optimizing a Trainium2 kernel written in Bass

```python
import math
import jax, jax.numpy as jnp
from jax import lax
import numpy as np

D_MODEL = 1024
BATCH = 1
SEQ = 512
DEPTH = 1

GRID_W = 64
HEAD_DIM = 64
ATTN_WIDTH = D_MODEL // 2
N_ATTN_HEADS = ATTN_WIDTH // HEAD_DIM
N_KV_HEADS = N_ATTN_HEADS // 4
KV_WIDTH = N_KV_HEADS * HEAD_DIM
SSM_WIDTH = D_MODEL // 2
SSM_HEAD_DIM = 64
SSM_HEADS = SSM_WIDTH // SSM_HEAD_DIM
SSM_GROUPS = 2
SSM_STATE = 128
SSM_CHUNK = 128
CONV_K = 5
XBC_WIDTH = SSM_WIDTH + 2 * SSM_GROUPS * SSM_STATE
D_MIX = ATTN_WIDTH + SSM_WIDTH
IN_SPLITS = (ATTN_WIDTH,
             ATTN_WIDTH + KV_WIDTH,
             ATTN_WIDTH + 2 * KV_WIDTH,
             ATTN_WIDTH + 2 * KV_WIDTH + SSM_WIDTH,
             ATTN_WIDTH + 2 * KV_WIDTH + SSM_WIDTH + XBC_WIDTH)
IN_WIDTH = IN_SPLITS[-1] + 2 * SSM_HEADS
Q_BLOCK = 128
ROPE_THETA = 10000.0
ROPE_AXIS_DIM = HEAD_DIM // 2
N_EXPERTS = 32
TOP_K = 4
D_EXPERT = D_MODEL
SWIGLU_LIMIT = 7.0
SWIGLU_ALPHA = 1.702
MOE_BLOCK = 128
EPS = 1e-6

kernel_name = "hymba_ssd_axial_gqa_moe_encoder"

def rms_norm(x, gain):
    xf = x.astype(jnp.float32)
    y = xf * lax.rsqrt(jnp.mean(xf * xf, axis=-1, keepdims=True) + EPS)
    return (y * gain.astype(jnp.float32)).astype(x.dtype)

def axial_rope_tables(seq_len):
    rows = seq_len // GRID_W
    row = jnp.repeat(jnp.arange(rows, dtype=jnp.float32), GRID_W)
    col = jnp.tile(jnp.arange(GRID_W, dtype=jnp.float32), rows)
    inv_freq = ROPE_THETA ** (-jnp.arange(0, ROPE_AXIS_DIM, 2, dtype=jnp.float32) / ROPE_AXIS_DIM)
    ang_r = row[:, None] * inv_freq
    ang_c = col[:, None] * inv_freq
    return jnp.cos(ang_r), jnp.sin(ang_r), jnp.cos(ang_c), jnp.sin(ang_c)

def rope_1d(x, cos, sin):
    x1, x2 = jnp.split(x, 2, axis=-1)
    c = cos[:, None, :].astype(x.dtype)
    s = sin[:, None, :].astype(x.dtype)
    return jnp.concatenate([x1 * c - x2 * s, x2 * c + x1 * s], axis=-1)

def axial_rope(x, tables):
    cr, sr, cc, sc = tables
    return jnp.concatenate([rope_1d(x[..., :ROPE_AXIS_DIM], cr, sr),
                            rope_1d(x[..., ROPE_AXIS_DIM:], cc, sc)], axis=-1)

def block_attention(q, k, v):
    b, l, h, d = q.shape
    g = h // N_KV_HEADS
    nb = l // Q_BLOCK
    scale = 1.0 / math.sqrt(d)
    qb = q.reshape(b, nb, Q_BLOCK, N_KV_HEADS, g, d).transpose(1, 0, 2, 3, 4, 5)

    def one_block(qi):
        s = jnp.einsum('bqkgd,bskd->bkgqs', qi, k).astype(jnp.float32) * scale
        p = jax.nn.softmax(s, axis=-1).astype(v.dtype)
        return jnp.einsum('bkgqs,bskd->bqkgd', p, v)

    o = lax.map(one_block, qb)
    return o.transpose(1, 0, 2, 3, 4, 5).reshape(b, l, h * d)

def ssd_chunked(x, dt, a, bm, cm):
    b, l, h, p = x.shape
    n = bm.shape[-1]
    c = l // SSM_CHUNK
    x = x.reshape(b, c, SSM_CHUNK, h, p)
    dt = dt.reshape(b, c, SSM_CHUNK, h)
    bm = bm.reshape(b, c, SSM_CHUNK, h, n)
    cm = cm.reshape(b, c, SSM_CHUNK, h, n)
    a_cum = jnp.cumsum(jnp.moveaxis(dt * a, 2, -1), axis=-1)
    xdt = x * dt[..., None]
    seg = a_cum[..., :, None] - a_cum[..., None, :]
    tri = jnp.tril(jnp.ones((SSM_CHUNK, SSM_CHUNK), dtype=bool))
    decay = jnp.exp(jnp.where(tri, seg, -jnp.inf))
    cb = jnp.einsum('bcqhn,bcshn->bchqs', cm, bm)
    y_diag = jnp.einsum('bchqs,bcshp->bcqhp', cb * decay, xdt)
    decay_to_end = jnp.exp(a_cum[..., -1:] - a_cum)
    states = jnp.einsum('bcshn,bchs,bcshp->bchpn', bm, decay_to_end, xdt)
    chunk_decay = jnp.exp(a_cum[..., -1])

    def step(carry, inp):
        st, dec = inp
        return carry * dec[..., None, None] + st, carry

    init = jnp.zeros((b, h, p, n), jnp.float32)
    _, prev = lax.scan(step, init, (jnp.moveaxis(states, 1, 0), jnp.moveaxis(chunk_decay, 1, 0)))
    prev = jnp.moveaxis(prev, 0, 1)
    y_off = jnp.einsum('bcqhn,bchpn,bchq->bcqhp', cm, prev, jnp.exp(a_cum))
    return (y_diag + y_off).reshape(b, l, h, p)

def ssm_branch(z, xbc, dt_raw, conv_w, conv_b, dt_bias, a_log, d_skip, norm_gain):
    b, l, _ = xbc.shape
    f32 = jnp.float32
    xbc = lax.conv_general_dilated(xbc, conv_w[:, None, :].astype(xbc.dtype), window_strides=(1,),
                                   padding=[(CONV_K // 2, CONV_K // 2)],
                                   dimension_numbers=('NWC', 'WIO', 'NWC'),
                                   feature_group_count=XBC_WIDTH) + conv_b
    xbc = jax.nn.silu(xbc)
    xs, bm, cm = jnp.split(xbc, [SSM_WIDTH, SSM_WIDTH + SSM_GROUPS * SSM_STATE], axis=-1)
    rep = SSM_HEADS // SSM_GROUPS
    xs = xs.reshape(b, l, SSM_HEADS, SSM_HEAD_DIM).astype(f32)
    bm = jnp.repeat(bm.reshape(b, l, SSM_GROUPS, SSM_STATE).astype(f32), rep, axis=2)
    cm = jnp.repeat(cm.reshape(b, l, SSM_GROUPS, SSM_STATE).astype(f32), rep, axis=2)
    dt = jax.nn.softplus(dt_raw.astype(f32).reshape(b, l, 2, SSM_HEADS) + dt_bias.astype(f32))
    a = -jnp.exp(a_log.astype(f32))
    y_fwd = ssd_chunked(xs, dt[:, :, 0], a[0], bm, cm)
    flip = lambda t: jnp.flip(t, axis=1)
    y_bwd = flip(ssd_chunked(flip(xs), flip(dt[:, :, 1]), a[1], flip(bm), flip(cm)))
    y = y_fwd + y_bwd + xs * d_skip.astype(f32)[:, None]
    y = y.reshape(b, l, SSM_WIDTH) * jax.nn.silu(z.astype(f32))
    y = rms_norm(y.reshape(b, l, SSM_GROUPS, SSM_WIDTH // SSM_GROUPS),
                 norm_gain.reshape(SSM_GROUPS, SSM_WIDTH // SSM_GROUPS))
    return y.reshape(b, l, SSM_WIDTH).astype(z.dtype)

def moe_ffn(h, w_router, b_router, w_gate, b_gate, w_up, b_up, w_down, b_down):
    b, l, d = h.shape
    t = h.reshape(-1, d)
    n_tok = t.shape[0]
    logits = (t @ w_router + b_router).astype(jnp.float32)
    top_val, top_idx = lax.top_k(logits, TOP_K)
    top_w = jax.nn.softmax(top_val, axis=-1)
    n_assign = n_tok * TOP_K
    flat_e = top_idx.reshape(-1)
    flat_tok = jnp.repeat(jnp.arange(n_tok, dtype=jnp.int32), TOP_K)
    flat_w = top_w.reshape(-1)
    counts = jnp.bincount(flat_e, length=N_EXPERTS)
    padded = (counts + MOE_BLOCK - 1) // MOE_BLOCK * MOE_BLOCK
    pad_end = jnp.cumsum(padded)
    pad_start = pad_end - padded
    start = jnp.cumsum(counts) - counts
    order = jnp.argsort(flat_e)
    sorted_e = flat_e[order]
    dest = pad_start[sorted_e] + jnp.arange(n_assign) - start[sorted_e]
    n_rows = n_assign + N_EXPERTS * MOE_BLOCK
    row_tok = jnp.zeros((n_rows,), jnp.int32).at[dest].set(flat_tok[order])
    row_w = jnp.zeros((n_rows,), jnp.float32).at[dest].set(flat_w[order])
    n_blocks = n_rows // MOE_BLOCK
    block_e = jnp.minimum(jnp.searchsorted(pad_end, jnp.arange(n_blocks) * MOE_BLOCK, side='right'),
                          N_EXPERTS - 1)
    xs = t[row_tok].reshape(n_blocks, MOE_BLOCK, d)

    def expert_block(args):
        xb, e = args
        g = xb @ w_gate[e] + b_gate[e]
        u = xb @ w_up[e] + b_up[e]
        g = jnp.minimum(g, SWIGLU_LIMIT)
        u = jnp.clip(u, -SWIGLU_LIMIT, SWIGLU_LIMIT)
        act = g * jax.nn.sigmoid(SWIGLU_ALPHA * g) * (u + 1.0)
        return act @ w_down[e] + b_down[e]

    ys = lax.map(expert_block, (xs, block_e)).reshape(n_rows, d)
    out = jnp.zeros_like(t).at[row_tok].add(ys * row_w[:, None].astype(t.dtype))
    return out.reshape(b, l, d)

def setup_inputs(seed: int = 0) -> dict:
    key = jax.random.key(seed)
    ks = jax.random.split(key, 24)
    f32 = jnp.float32
    nrm = lambda k, shape, s: jax.random.normal(k, shape, f32) * s
    gain = lambda k, shape: 1.0 + 0.02 * jax.random.normal(k, shape, f32)
    dt0 = jnp.exp(jax.random.uniform(ks[7], (DEPTH, 2, SSM_HEADS), f32) * (math.log(0.1) - math.log(0.001)) + math.log(0.001))
    return {
        "x": nrm(ks[0], (BATCH, SEQ, D_MODEL), 1.0),
        "norm_mix": gain(ks[1], (DEPTH, D_MODEL)),
        "w_in": nrm(ks[2], (DEPTH, D_MODEL, IN_WIDTH), D_MODEL ** -0.5),
        "q_norm": gain(ks[3], (DEPTH, HEAD_DIM)),
        "k_norm": gain(ks[4], (DEPTH, HEAD_DIM)),
        "conv_w": nrm(ks[5], (DEPTH, CONV_K, XBC_WIDTH), CONV_K ** -0.5),
        "conv_b": nrm(ks[6], (DEPTH, XBC_WIDTH), 0.02),
        "dt_bias": dt0 + jnp.log(-jnp.expm1(-dt0)),
        "a_log": jnp.log(jax.random.uniform(ks[8], (DEPTH, 2, SSM_HEADS), f32, 1.0, 16.0)),
        "d_skip": gain(ks[9], (DEPTH, SSM_HEADS)),
        "ssm_norm": gain(ks[10], (DEPTH, SSM_WIDTH)),
        "attn_norm": gain(ks[11], (DEPTH, ATTN_WIDTH)),
        "w_out": nrm(ks[12], (DEPTH, D_MIX, D_MODEL), D_MIX ** -0.5),
        "norm_ffn": gain(ks[13], (DEPTH, D_MODEL)),
        "w_router": nrm(ks[14], (DEPTH, D_MODEL, N_EXPERTS), D_MODEL ** -0.5),
        "b_router": nrm(ks[15], (DEPTH, N_EXPERTS), 0.01),
        "w_gate": nrm(ks[16], (DEPTH, N_EXPERTS, D_MODEL, D_EXPERT), D_MODEL ** -0.5),
        "b_gate": nrm(ks[17], (DEPTH, N_EXPERTS, D_EXPERT), 0.01),
        "w_up": nrm(ks[18], (DEPTH, N_EXPERTS, D_MODEL, D_EXPERT), D_MODEL ** -0.5),
        "b_up": nrm(ks[19], (DEPTH, N_EXPERTS, D_EXPERT), 0.01),
        "w_down": nrm(ks[20], (DEPTH, N_EXPERTS, D_EXPERT, D_MODEL), D_EXPERT ** -0.5),
        "b_down": nrm(ks[21], (DEPTH, N_EXPERTS, D_MODEL), 0.01),
    }

def reference(x, norm_mix, w_in, q_norm, k_norm, conv_w, conv_b, dt_bias, a_log, d_skip,
              ssm_norm, attn_norm, w_out, norm_ffn, w_router, b_router, w_gate, b_gate,
              w_up, b_up, w_down, b_down):
    b, l, _ = x.shape
    rope = axial_rope_tables(l)
    for i in range(DEPTH):
        hn = rms_norm(x, norm_mix[i])
        proj = hn @ w_in[i]
        q, k, v, z, xbc, dt_raw = jnp.split(proj, IN_SPLITS, axis=-1)
        q = axial_rope(rms_norm(q.reshape(b, l, N_ATTN_HEADS, HEAD_DIM), q_norm[i]), rope)
        k = axial_rope(rms_norm(k.reshape(b, l, N_KV_HEADS, HEAD_DIM), k_norm[i]), rope)
        v = v.reshape(b, l, N_KV_HEADS, HEAD_DIM)
        attn = rms_norm(block_attention(q, k, v), attn_norm[i])
        ssm = ssm_branch(z, xbc, dt_raw, conv_w[i], conv_b[i], dt_bias[i], a_log[i],
                         d_skip[i], ssm_norm[i])
        x = x + jnp.concatenate([attn, ssm], axis=-1) @ w_out[i]
        x = x + moe_ffn(rms_norm(x, norm_ffn[i]), w_router[i], b_router[i], w_gate[i], b_gate[i],
                        w_up[i], b_up[i], w_down[i], b_down[i])
    return x


_drawn_inputs = setup_inputs


def setup_inputs(seed=0):
    import zlib

    import numpy as np

    out = dict(_drawn_inputs(seed))
    spreads = {}
    factors = {'d_skip': 13.317, 'b_router': 2.782, 'b_gate': 8.0, 'b_up': 24.381, 'b_down': 8.0}
    for name, (base, spread) in spreads.items():
        noise = np.random.default_rng([zlib.crc32(name.encode()), seed]).standard_normal(out[name].shape)
        drawn = base * np.exp(spread * noise) if base else spread * noise
        out[name] = __import__('jax').numpy.asarray(drawn.astype(out[name].dtype))
    for name, factor in factors.items():
        out[name] = (out[name] * factor).astype(out[name].dtype)
    return out
```

```python
import concourse.bass as bass
from concourse import mybir
from contextlib import ExitStack
import numpy as np

F32 = mybir.dt.float32
I32 = mybir.dt.int32
U32 = mybir.dt.uint32
ALU = mybir.AluOpType
ACT = mybir.ActivationFunctionType
AX = mybir.AxisListType

P = 128
SEQ, DM = 512, 1024
NT = SEQ // P
KT = DM // P
HD = 64
NH, NKV = 8, 2
SH, SG, SN = 8, 2, 128
HPG = SH // SG
AW = NH * HD
KVW = NKV * HD
SW = SH * HD
GW = SW // SG
XBC = SW + 2 * SG * SN
CONV = 5
Z0 = AW + 2 * KVW
XBC0 = Z0 + SW
DT0 = XBC0 + XBC
INW = DT0 + 2 * SH
CT = XBC // P
NE, TOPK = 32, 4
DE = DM
EPS = 1e-6
LIMIT, ALPHA = 7.0, 1.702
GRID_W = 64
IW = 52
MAX_ITEMS = NE + SEQ * TOPK // P
FAR = 8192.0
HALF = DE // 2
SLOTS = 6
SLOT = KT * HALF

C_LE, C_GE, C_GT, C_LT, C_ID, C_ONE, C_IOTA = (n * P for n in range(7))
C_COS = 7 * P
C_SIN = C_COS + NT * HD
C_EPS = C_SIN + NT * HD
C_ROW = C_EPS + 1
C_TOK = C_ROW + 1
C_END = C_TOK + NT


def constants():
    f = np.float32
    t, q = np.arange(P)[:, None], np.arange(P)[None, :]
    c = np.zeros((P, C_END), f)
    for at, m in ((C_LE, t <= q), (C_GE, t >= q), (C_GT, t > q), (C_LT, t < q), (C_ID, t == q)):
        c[:, at:at + P] = m
    c[:, C_ONE:C_ONE + P] = 1
    c[:, C_IOTA:C_IOTA + P] = q
    half = HD // 2
    inv = (f(10000.0) ** (-np.arange(0, half, 2, dtype=f) / f(half))).astype(f)
    tok = np.arange(SEQ)
    ar = (tok // GRID_W).astype(f)[:, None] * inv
    ac = (tok % GRID_W).astype(f)[:, None] * inv
    cos = np.concatenate([np.cos(ar), np.cos(ar), np.cos(ac), np.cos(ac)], 1).astype(f)
    sin = np.concatenate([-np.sin(ar), np.sin(ar), -np.sin(ac), np.sin(ac)], 1).astype(f)
    c[:, C_COS:C_SIN] = cos.reshape(NT, P, HD).transpose(1, 0, 2).reshape(P, -1)
    c[:, C_SIN:C_EPS] = sin.reshape(NT, P, HD).transpose(1, 0, 2).reshape(P, -1)
    c[:, C_EPS] = EPS
    c[:, C_ROW] = np.arange(P)
    c[:, C_TOK:C_END] = np.arange(P)[:, None] + P * np.arange(NT)
    return c


def units():
    u = ["par"] + [f"xT{t}{h}" for t in range(NT) for h in "ab"] + ["bg", "bu", "bd", "dt"]
    u += [f"xb{ch}" for ch in CHANNELS]
    u += ["q0", "kv0", "q1", "kv1"] + [f"cs{c}" for c in range(NT)] + ["tq0", "tk0"]
    for c in range(NT):
        u += [f"tx{c}", f"tb{c}"]
    u += ["q2", "kv2", "tq1", "tk1", "q3", "kv3", "z0", "z1", "tq2", "tk2"] + decay_units(0)
    u += ["z2", "z3", "tq3", "tk3"]
    for c in range(NT):
        u += decay_units(c + 1) + [f"yd{c}"] + [f"sf{c}"] * (c < NT - 1) + [f"sb{c}"] * (c > 0)
    for s in range(STEPS):
        if s < NPAIR:
            u += [f"s{s}a", f"s{s}b"]
        if 1 <= s <= NPAIR:
            u += [f"p{s - 1}a", f"p{s - 1}b"]
        if s % 4 == 3 and s < NPAIR:
            u += [f"yf{s // 4}"] * (s // 4 > 0) + [f"yb{s // 4}"] * (s // 4 < NT - 1)
        for first, name, parts in ((TM, "tm", "ab"), (OP, "op", "ab"), (TH, "th", "ab"), (LG, "lg", " ")):
            if turn_at(s, first) is not None:
                u += [f"{name}{turn_at(s, first)}{h}".strip() for h in parts]
    return u + ["cum", "tab"]


def decay_units(c):
    return [f"cb{c}"] + [f"sg{c}{d}{g}" for d in "fb" for g in range(SG)] if c < NT else []


CHANNELS = (6, 7, 4, 5, 0, 1, 2, 3)
NPAIR = NT * NH // 2
TM, OP, TH, LG = 7, 8, 10, 11
STEPS = LG + 4 * (NT - 1) + 1


def turn_at(s, first):
    t, r = divmod(s - first, 4)
    return t if r == 0 and 0 <= t < NT else None


def hybrid_layer(nc, d, out, hn):
    ctx = ExitStack()
    with ctx:
        def sem(name):
            return ctx.enter_context(nc.semaphore(name))

        ring = ctx.enter_context(nc.sbuf_tensor("ring", [P, SLOTS * SLOT], F32))
        REST = 28600
        rest = ctx.enter_context(nc.sbuf_tensor("rest", [P, REST], F32))
        at = [0]

        def take(n):
            at[0] += n
            assert at[0] <= REST, at[0]
            return rest[:, at[0] - n:at[0]]

        def cut(ap, *sizes):
            names = "abcd"[:len(sizes)]
            return ap.rearrange(f"p ({' '.join(names)}) -> p {' '.join(names)}", **dict(zip(names, sizes)))

        const = take(C_END)
        c_le, c_ge, c_gt, c_lt, ident, ones, iota = (const[:, n * P:(n + 1) * P] for n in range(7))
        cos_t = cut(const[:, C_COS:C_SIN], NT, HD)
        sin_t = cut(const[:, C_SIN:C_EPS], NT, HD)
        eps_c, row_c, tok_c = const[:, C_EPS:C_EPS + 1], const[:, C_ROW:C_ROW + 1], const[:, C_TOK:C_END]
        one_c = ones[:, 0:1]
        dtb, alog, dsk = take(2 * SH), take(2 * SH), take(SH)
        gains = take((NH + NKV) * HD)
        brow = take(NE)
        NPAR = 8 + 8 + CONV * CT + 4 + 4
        pcol = take(NPAR)
        pc_mix, pc_cb, pc_cw = pcol[:, 0:8], pcol[:, 8:16], pcol[:, 16:16 + CONV * CT]
        pc_att, pc_ssm = pcol[:, 56:60], pcol[:, 60:64]
        bias3 = [take(NE * KT) for _ in range(3)]
        work = at[0]
        hTm = cut(take(KT * SEQ), KT, SEQ)
        xsb_w = take(NT * DM)
        xsb = cut(xsb_w, NT, DM)
        sm = [cut(xsb_w[:, n * 512:n * 512 + 512], HPG, P) for n in range(2)]
        eseg = [cut(xsb_w[:, 1024 + n * 512:1536 + n * 512], HPG, P) for n in range(2)]
        gdec = [cut(xsb_w[:, 2048 + n * 512:2560 + n * 512], HPG, P) for n in range(4)]
        probs = [xsb_w[:, n * 512:n * 512 + 512] for n in range(4)]
        probsT = [cut(xsb_w[:, 2048 + n * 512:2560 + n * 512], NT, P) for n in range(4)]
        xc_w = take(CT * SEQ)
        xc = cut(xc_w, CT, SEQ)
        zs = cut(take(NT * SW), NT, SW)
        vs_w = take(NT * KVW)
        vs = cut(vs_w, NT, KVW)
        payload = cut(vs_w[:, 0:NT * NE * 3], NT, NE, 3)
        posm = cut(vs_w[:, NT * NE * 3:NT * NE * 4], NT, NE)
        qT = cut(take(NH // 2 * SEQ), NH // 2, SEQ)
        kT = cut(take(NKV * SEQ), NKV, SEQ)
        xs = cut(take(NT * SW), NT, SW)
        br_w = take(NT * SG * SN)
        brows = cut(br_w, NT, SG * SN)
        gffn = br_w
        xpad_w = take(2 * (SEQ + CONV - 1))
        xpad = cut(xpad_w, 2, SEQ + CONV - 1)
        ytmp = [xpad_w[:, n * 512:n * 512 + 512] for n in range(2)]
        QKW = (NH + NKV) * HD
        qk_w = take(3 * QKW + 2 * KVW)
        qk, qk2, qk3 = (qk_w[:, n * QKW:(n + 1) * QKW] for n in range(3))
        kd = cut(qk_w[:, 3 * QKW:], NKV, 2, HD)
        mixa, mixs, junk = (qk_w[:, n * 512:n * 512 + 512] for n in range(3))
        ssq = take(NT); rstd = take(NT)
        dtr = cut(take(NT * 16), NT, 16); dta = cut(take(NT * 16), NT, 16)
        dtv = cut(take(NT * 16), NT, 16); da = cut(take(NT * 16), NT, 16)
        ex = cut(take(NT * 48), NT, 48)
        qss = take(10); qrs = take(10)
        nb = [take(2) for _ in range(2)]
        sums = cut(take(2 * NH), 2, NH); rsum = take(NH)
        nss = cut(take(3 * 8), 3, 8); nrs = cut(take(3 * 8), 3, 8)
        lg = cut(take(NT * NE), NT, NE)
        m8 = cut(take(NT * 8), NT, 8); ix8 = cut(take(NT * 8), NT, 8); ixf = cut(take(NT * 8), NT, 8)
        nmx = take(NT); ws = cut(take(NT * TOPK), NT, TOPK); wsum = take(NT); wrec = take(NT)
        items_f = cut(take(3 * IW), 3, IW)
        items_i = cut(take(2 * IW), 2, IW)
        cum_i = take(NE)
        dsp = take(4); idx_g = take(1); idx_s = take(1); w_s = take(1); tmp1 = take(1)
        back = at[0]
        at[0] = work
        hrow = take(DM)
        hT = cut(take(DM), KT, P)
        actT = cut(take(DM), KT, P)
        yT = cut(take(DM), KT, P)
        yrow = take(DM)
        gb, ub, tb, sg = (cut(take(512), 4, P) for _ in range(4))
        onehot = cut(take(NT * P), NT, P)
        at[0] = back
        rt = zs.rearrange("p a b -> p (a b)").rearrange("p (a b) -> p a b", b=P)
        oh = [cut(rt[:, n, :], NT, NE) for n in range(4)]
        msk, wgt, tmpr = (cut(rt[:, n, :], NT, NE) for n in (4, 5, 6))
        cnt, nch, cume, cums, ohi, are = (rt[:, 7, n * 32:n * 32 + 32] if n < 4 else rt[:, 8, (n - 4) * 32:(n - 4) * 32 + 32] for n in range(6))
        icol = rt[:, 9, 0:4]
        rhs3 = cut(rt[:, 10:12, :].rearrange("p a b -> p (a b)")[:, 0:3 * IW], 3, IW)
        itm = rt[:, 12, 0:32]
        w_in = cut(ring[:, 0:KT * INW], KT, INW)
        x1 = cut(ring[:, SLOT:2 * SLOT], NT, DM)
        prev_w = ring[:, 2 * SLOT:2 * SLOT + 3072]
        prevf = {c: prev_w[:, (c - 1) * 512:c * 512] for c in (1, 2, 3)}
        prevb = {c: prev_w[:, 1536 + c * 512:2048 + c * 512] for c in (0, 1, 2)}
        ydsb = cut(ring[:, 2 * SLOT + 3072:2 * SLOT + 5120], NT, SW)
        w_out = cut(ring[:, 13312:21504], KT, DM)
        ta = ring[:, 21504:23552]
        xn = cut(ta, 2, DM)
        xdtf, xdtb, xwf, xwb = (ta[:, n * 512:n * 512 + 512] for n in range(4))
        hrw = ta[:, 0:DM]
        hrT = cut(ta[:, DM:2 * DM], KT, P)
        sgx = [ring[:, 23552 + n * 512:24064 + n * 512] for n in range(2)]
        cbm = cut(ring[:, 23552:24064], 2, SG * P)
        wr = cut(ring[:, 24064:24064 + KT * NE], KT, NE)
        slot = [cut(ring[:, s * SLOT:(s + 1) * SLOT], KT, HALF) for s in range(SLOTS)]
        praw = hTm[:, 0, 0:P]
        junkx = qT.rearrange("p a b -> p (a b)")[:, 0:DM]
        braw = [cut(vz, 2, P) for vz in (xc_w[:, 0:256], xc_w[:, 256:512], xc_w[:, 512:768])]

        bank = [ctx.enter_context(nc.psum_tensor(f"bank{n}", [P, 512], F32)) for n in range(8)]
        RINGB = 7
        order = units()
        where = {u: divmod(n, RINGB) for n, u in enumerate(order)}
        assert len(where) == len(order)
        psum_full = [sem(f"psum_full{n}") for n in range(RINGB)]
        psum_free = [sem(f"psum_free{n}") for n in range(RINGB)]

        def wait_full(eng, u):
            turn, b = where[u]
            eng.wait_ge(psum_full[b], turn + 1)
            return bank[b]

        def freed(ins, u):
            ins.then_inc(psum_free[where[u][1]], 1)

        def wait_taken(eng, u):
            turn, b = where[u]
            eng.wait_ge(psum_free[b], turn + 1)

        s_const, s_par, s_rows, s_bias = sem("const_in"), sem("par_in"), sem("rows_in"), sem("bias_in")
        s_x = [sem(f"x{t}_in") for t in range(NT)]
        s_win = [sem(f"w_in{n}_in") for n in range(3)]
        s_wout, s_wr, s_gffn = sem("w_out_in"), sem("w_router_in"), sem("gain_ffn_in")
        s_xr = [sem(f"x{t}_again") for t in range(NT)]
        s_rstd, s_xn, s_pad0 = sem("rstd_ready"), sem("xn_ready"), sem("pads_zeroed")
        s_act, s_dve = sem("act_chain"), sem("dve_chain")
        s_conv, s_sgx, s_xc = sem("conv_ready"), sem("conv_sigmoid"), sem("xc_ready")
        s_dta, s_dtl, s_da = sem("dt_abs"), sem("dt_log"), sem("da_ready")
        s_sm, s_g = sem("scaled_mask"), sem("decay_ready")
        s_xdt, s_prev = sem("xdt_ready"), sem("prev_ready")
        s_qss, s_qrs, s_rot = sem("qk_copied"), sem("qk_rstd"), sem("qk_rotated")
        s_qsq = sem("qk_squares")
        s_zsig = sem("z_sigmoid")
        s_nb = sem("row_max")
        s_of, s_ofree = sem("attn_full"), sem("attn_taken")
        s_ys, s_yn = sem("ssd_rows"), sem("ssd_rstd")
        s_an = sem("attn_rstd")
        s_mixa, s_mixs = sem("mix_attn"), sem("mix_ssd")
        s_x1n, s_h = sem("x1_rstd"), sem("h_ready")
        s_hst, s_ost = sem("h_stored"), sem("x1_stored")
        s_rt, s_rte, s_tabr, s_cnt = sem("logit_max"), sem("weights_exp"), sem("table_cols"), sem("mask_ready")
        s_tab = sem("tables_ready")
        s_full = [sem(f"slot{n}_in") for n in range(SLOTS)]
        s_uc, s_tb, s_i1, s_i2 = sem("up_clamped"), sem("gate_up"), sem("dispatch_copied"), sem("index_part")
        s_oh, s_dsp, s_idx, s_gath = sem("onehot_ready"), sem("dispatch_full"), sem("index_ready"), sem("gathered")
        s_tin, s_hT = sem("rows_transposed"), sem("hT_ready")
        s_used = [sem(f"slot{n}_used") for n in range(SLOTS)]
        s_gt, s_ut = sem("gate_taken"), sem("up_taken")
        s_gb, s_sg, s_at = sem("gate_clamped"), sem("gate_sigmoid"), sem("act_ready")
        s_yt = sem("yT_ready")
        s_yf, s_ws, s_y, s_scat = sem("y_transposed"), sem("weight_ready"), sem("y_ready"), sem("scattered")
        s_landed, s_moves = sem("additions_landed"), sem("row_moves_begun")

        w_in_d = d["w_in"][0].rearrange("(k p) n -> p k n", p=P)
        w_out_d = d["w_out"][0].rearrange("(k p) n -> p k n", p=P)
        x_d = d["x"][0].rearrange("(t p) n -> t p n", p=P)
        out_d = out[0]
        hn_d = hn

        def bc(row, n=P):
            return row.partition_broadcast(n)

        def over(ap, k):
            return ap.unsqueeze(2).to_broadcast([P, ap.shape[1], k])

        def times(ap, k):
            return ap.unsqueeze(1).to_broadcast([P, k, ap.shape[1]])

        def slot_source(s, e):
            w = d[("w_gate", "w_up", "w_gate", "w_up", "w_down", "w_down")[s]]
            h = (0, 0, 1, 1, 0, 1)[s]
            return w[0, e].rearrange("(k p) n -> p k n", p=P)[:, :, h * HALF:(h + 1) * HALF]

        block = ctx.enter_context(nc.Block())

        @block.sync
        def _(sp):
            sp.dma_start(const, d["const"]).then_inc(s_const, 16)
            for t in range(NT):
                sp.dma_start(xsb[:, t, :], x_d[t]).then_inc(s_x[t], 16)
            for n, (a, b) in enumerate(((XBC0, INW), (0, Z0), (Z0, XBC0))):
                sp.dma_start(w_in[:, :, a:b], w_in_d[:, :, a:b]).then_inc(s_win[n], 16)
            wait_full(sp, f"z{NT - 1}")
            for t in range(NT):
                sp.dma_start(x1[:, t, :], x_d[t]).then_inc(s_xr[t], 16)
            sp.dma_start(w_out, w_out_d).then_inc(s_wout, 16)
            sp.dma_start(wr, d["w_router"][0].rearrange("(k p) n -> p k n", p=P)).then_inc(s_wr, 16)
            sp.dma_start(slot[0], slot_source(0, 0)).then_inc(s_full[0], 16)
            wait_full(sp, f"sb{NT - 1}")
            sp.dma_start(gffn, bc(d["norm_ffn"][0])).then_inc(s_gffn, 16)
            for t in range(NT):
                wait_taken(sp, f"op{t}a")
                wait_taken(sp, f"op{t}b")
                sp.dma_start(out_d[t * P:(t + 1) * P, :], x1[:, t, :]).then_inc(s_ost, 16)
                sp.wait_ge(s_h, t + 1)
                sp.dma_start(hn_d[t * P:(t + 1) * P, :], hrw).then_inc(s_hst, 16)
            wait_taken(sp, f"lg{NT - 1}")
            sp.wait_ge(s_hst, 16 * NT)
            sp.wait_ge(s_ost, 16 * NT)
            for s in range(1, SLOTS):
                sp.dma_start(slot[s], slot_source(s, 0)).then_inc(s_full[s], 16)
            sp.wait_ge(s_tab, 1)
            with sp.Fori(1, NE) as e:
                before = sp.value_load(cum_i[0:1, bass.ds(e - 1, 1)].bitcast(I32), min_val=1, max_val=MAX_ITEMS)
                for s in range(SLOTS):
                    sp.wait_ge(s_used[s], before)
                    sp.dma_start(slot[s], slot_source(s, e)).then_inc(s_full[s], 16)

        @block.gpsimd
        def _(pool):
            k = 0
            pool.wait_ge(s_da, 1)
            pool.wait_ge(s_const, 16)
            for c in range(NT):
                for di, mask in enumerate((c_gt, c_lt)):
                    for g in range(SG):
                        if k >= 2:
                            n = k - 2
                            wait_full(pool, f"sg{n // 4}{'fb'[n // 2 % 2]}{n % 2}")
                        elif k == 0:
                            wait_full(pool, f"xT{NT - 1}b")
                        nc.gpsimd.tensor_tensor(
                            out=sm[k % 2], in0=times(mask, HPG),
                            in1=over(da[:, c, di * SH + g * HPG:di * SH + (g + 1) * HPG], P),
                            op=ALU.mult).then_inc(s_sm, 1)
                        k += 1
            pool.wait_ge(s_hst, 16 * NT)
            pool.wait_ge(s_ost, 16 * NT)
            pool.wait_ge(s_tab, 1)
            pool.wait_ge(s_idx, 1)

            def gather():
                nc.gpsimd.indirect_dma_start(
                    out=hrow, out_offset=None, in_=hn_d,
                    in_offset=bass.IndirectOffsetOnAxis(ap=idx_g.bitcast(I32), axis=0),
                    bounds_check=SEQ - 1, oob_is_err=False).then_inc(s_gath, 16)

            gather()
            pool.sem_inc(s_landed, 1)
            nitems = pool.value_load(cum_i[0:1, NE - 1:NE].bitcast(I32), min_val=NE, max_val=MAX_ITEMS)
            with pool.Fori(0, MAX_ITEMS) as i:
                with pool.If(i < nitems):
                    pool.wait_ge(s_idx, i + 2)
                    pool.wait_ge(s_tin, i + 1)
                    pool.sem_inc(s_moves, 1)
                    gather()
                    pool.wait_ge(s_y, 2 * i + 3)
                    pool.sem_inc(s_moves, 1)
                    nc.gpsimd.indirect_dma_start(
                        out=out_d, out_offset=bass.IndirectOffsetOnAxis(ap=idx_s.bitcast(I32), axis=0),
                        in_=yrow, in_offset=None, bounds_check=SEQ - 1, oob_is_err=False,
                        compute_op=ALU.add).then_inc(s_scat, 16)
                    pool.wait_ge(s_scat, 16 * i + 16)
                    pool.sem_inc(s_landed, 1)

        @block.scalar
        def _(act):
            chain = [0]

            def link(ins):
                chain[0] += 1
                ins.then_inc(s_act, 1)
                act.wait_ge(s_act, chain[0])

            for name, r0, n in (("norm_mix", 0, 8), ("conv_b", 8, 8), ("conv_w", 16, 40),
                                ("attn_norm", 56, 4), ("ssm_norm", 60, 4)):
                src = d[name][0]
                if name == "conv_w":
                    src = src.rearrange("k (c p) -> (k c) p", p=P)
                else:
                    src = src.rearrange("(c p) -> c p", p=P)
                act.dma_start(praw[r0:r0 + n, :], src).then_inc(s_par, 16)
            for dst, src in ((dtb, d["dt_bias"][0].rearrange("a h -> (a h)")),
                             (alog, d["a_log"][0].rearrange("a h -> (a h)")),
                             (dsk, d["d_skip"][0]), (brow, d["b_router"][0]),
                             (qk[:, 0:HD], d["q_norm"][0]), (qk[:, HD:2 * HD], d["k_norm"][0])):
                act.dma_start(dst, bc(src)).then_inc(s_rows, 16)
            for b, name in zip(braw, ("b_gate", "b_up", "b_down")):
                act.dma_start(b, d[name][0].rearrange("(a e) (t p) -> (e t) a p", a=2, p=P)).then_inc(s_bias, 16)

            def rms(out, ss, n):
                link(nc.scalar.activation(out, ss, ACT.Ln, scale=1.0 / n, bias=eps_c))
                return nc.scalar.activation(out, out, ACT.Exp, scale=-0.5)

            act.wait_ge(s_const, 16)
            for t in range(NT):
                act.wait_ge(s_x[t], 16)
                link(nc.scalar.activation(junkx, xsb[:, t, :], ACT.Square, accum_out=ssq[:, t:t + 1]))
                rms(rstd[:, t:t + 1], ssq[:, t:t + 1], DM).then_inc(s_rstd, 1)
            act.wait_ge(s_rows, 16 * 6)
            link(nc.scalar.activation(alog, alog, ACT.Exp))
            act.wait_ge(s_dta, 1)
            link(nc.scalar.activation(dta, dta, ACT.Exp, scale=-1.0))
            nc.scalar.activation(dta, dta, ACT.Ln, bias=one_c).then_inc(s_dtl, 1)
            act.wait_ge(s_pad0, 1)
            def conv_sigmoid(n):
                act.wait_ge(s_conv, n + 1)
                if n >= 2:
                    act.wait_ge(s_xc, n - 1)
                nc.scalar.activation(sgx[n % 2], xc[:, CHANNELS[n], :], ACT.Sigmoid).then_inc(s_sgx, 1)

            for n, ch in enumerate(CHANNELS):
                if n >= 2:
                    act.wait_ge(s_conv, n - 1)
                ps = wait_full(act, f"xb{ch}")
                freed(nc.scalar.activation(xpad[:, n % 2, 2:2 + SEQ], ps[:, :], ACT.Copy), f"xb{ch}")
                if n:
                    conv_sigmoid(n - 1)
            conv_sigmoid(CT - 1)

            def copy_out(u, dst, n=512):
                ps = wait_full(act, u)
                src = ps[:, 0:n]
                if len(dst.shape) == 3:
                    src = cut(src, dst.shape[1], dst.shape[2])
                freed(nc.scalar.activation(dst, src, ACT.Copy), u)

            def take_qkv(t):
                act.wait_ge(s_qss, 1)
                if t:
                    act.wait_ge(s_rot, t)
                copy_out(f"q{t}", qk[:, 0:AW])
                ps = wait_full(act, f"kv{t}")
                link(nc.scalar.activation(qk[:, AW:QKW], ps[:, 0:KVW], ACT.Copy))
                freed(nc.scalar.activation(vs[:, t, :], ps[:, KVW:2 * KVW], ACT.Copy), f"kv{t}")
                wait_taken(act, f"q{t}")
                nc.scalar.activation(qk2, qk, ACT.Square).then_inc(s_qsq, 1)
                act.wait_ge(s_qss, t + 2)
                rms(qrs, qss, HD).then_inc(s_qrs, 1)

            def take_heads(t):
                copy_out(f"tq{t}", qT[:, :, t * P:(t + 1) * P])
                copy_out(f"tk{t}", kT[:, :, t * P:(t + 1) * P], NKV * P)

            seg = [0]

            def decays(c):
                if c == NT:
                    return
                for di in "fb":
                    for g in range(SG):
                        k = seg[0]
                        if k >= 2:
                            act.wait_ge(s_g, k - 1)
                        elif k == 0:
                            wait_full(act, f"xT{NT - 1}b")
                        copy_exp = f"sg{c}{di}{g}"
                        ps = wait_full(act, copy_exp)
                        freed(nc.scalar.activation(eseg[k % 2], cut(ps[:, :], HPG, P), ACT.Exp), copy_exp)
                        seg[0] += 1

            take_qkv(0)
            take_qkv(1)
            for c in range(NT):
                ps = wait_full(act, f"cs{c}")
                freed(nc.scalar.activation(ex[:, c, :], ps[:, 0:48], ACT.Exp), f"cs{c}")
            take_heads(0)
            for c in range(NT):
                copy_out(f"tx{c}", xs[:, c, :])
                copy_out(f"tb{c}", brows[:, c, :], SG * SN)
            take_qkv(2)
            take_heads(1)
            take_qkv(3)
            copy_out("z0", zs[:, 0, :])
            copy_out("z1", zs[:, 1, :])
            take_heads(2)
            decays(0)
            copy_out("z2", zs[:, 2, :])
            copy_out("z3", zs[:, 3, :])
            take_heads(3)
            for c in range(NT):
                decays(c + 1)
                copy_out(f"yd{c}", ydsb[:, c, :])
            for c in range(NT):
                nc.scalar.activation(xc[:, c, :], zs[:, c, :], ACT.Sigmoid).then_inc(s_zsig, 1)

            for s in range(STEPS):
                if s < NPAIR:
                    act.wait_ge(s_nb, s + 1)
                    if s >= 2:
                        wait_full(act, f"p{s - 2}b")
                    for h in range(2):
                        ps = wait_full(act, f"s{s}{'ab'[h]}")
                        head = s % 4 * 2 + h
                        freed(nc.scalar.activation(probs[s % 2 * 2 + h], ps[:, :], ACT.Exp, scale=HD ** -0.5,
                                                   bias=nb[s % 2][:, h:h + 1],
                                                   accum_out=sums[:, s // 4 % 2, head:head + 1]), f"s{s}{'ab'[h]}")
                if 1 <= s <= NPAIR:
                    n = s - 1
                    if n >= 2:
                        act.wait_ge(s_of, n - 1)
                    ps = wait_full(act, f"p{n}a")
                    freed(nc.scalar.activation(probsT[n % 2 * 2], cut(ps[:, :], NT, P), ACT.Copy), f"p{n}a")
                if turn_at(s, 5) is not None:
                    i = turn_at(s, 5)
                    act.wait_ge(s_ofree, i + 1)
                    link(nc.scalar.activation(junk, mixa, ACT.Square, accum_out=nss[:, 0, i:i + 1]))
                    rms(nrs[:, 0, i:i + 1], nss[:, 0, i:i + 1], AW).then_inc(s_an, 1)
                if turn_at(s, 3) is not None:
                    i = turn_at(s, 3)
                    act.wait_ge(s_ys, i + 1)
                    for g in range(SG):
                        col = i * SG + g
                        link(nc.scalar.activation(junk[:, 0:GW], mixs[:, g * GW:(g + 1) * GW], ACT.Square,
                                                  accum_out=nss[:, 1, col:col + 1]))
                    rms(nrs[:, 1, i * SG:(i + 1) * SG], nss[:, 1, i * SG:(i + 1) * SG], GW).then_inc(s_yn, 1)
                if turn_at(s, OP) is not None:
                    t = turn_at(s, OP)
                    wait_taken(act, f"op{t}a")
                    wait_taken(act, f"op{t}b")
                    if t:
                        wait_full(act, f"lg{t - 1}")
                    else:
                        wait_full(act, f"sb{NT - 1}")
                    link(nc.scalar.activation(hrT.rearrange("p a b -> p (a b)"), x1[:, t, :], ACT.Square,
                                              accum_out=nss[:, 2, t:t + 1]))
                    rms(nrs[:, 2, t:t + 1], nss[:, 2, t:t + 1], DM).then_inc(s_x1n, 1)
                if turn_at(s, TH) is not None:
                    t = turn_at(s, TH)
                    for h in range(2):
                        copy_out(f"th{t}{'ab'[h]}", hrT[:, 4 * h:4 * h + 4, :])
            act.wait_ge(s_rt, 1)
            for t in range(NT):
                nc_w = nc.scalar.activation(ws[:, t, :], m8[:, t, 0:TOPK], ACT.Exp, bias=nmx[:, t:t + 1],
                                            accum_out=wsum[:, t:t + 1])
                nc_w.then_inc(s_rte, 1)

            def take_rows():
                for h in range(2):
                    ins = nc.scalar.activation(hT[:, 4 * h:4 * h + 4, :], cut(bank[4 + h][:, :], 4, P), ACT.Copy)
                return ins

            act.wait_ge(s_tab, 1)
            act.wait_ge(s_tin, 1)
            take_rows().then_inc(s_hT, 1)
            act.sem_inc(s_y, 1)
            nitems = act.value_load(cum_i[0:1, NE - 1:NE].bitcast(I32), min_val=NE, max_val=MAX_ITEMS)
            with act.Fori(0, MAX_ITEMS) as i:
                with act.If(i < nitems):
                    for h in range(2):
                        act.wait_ge(s_gb, 2 * i + h + 1)
                        act.wait_ge(s_at, 2 * i + h + 1)
                        nc.scalar.activation(sg, gb, ACT.Sigmoid, scale=ALPHA).then_inc(s_sg, 1)
                    act.wait_ge(s_tin, i + 2)
                    take_rows().then_inc(s_hT, 1)
                    act.wait_ge(s_ws, i + 1)
                    act.wait_ge(s_landed, i + 1)
                    act.wait_ge(s_yf, i + 2)
                    for h in range(2):
                        nc.scalar.activation(yrow[:, h * 512:h * 512 + 512], bank[6 + h][:, :], ACT.Copy,
                                             scale=w_s).then_inc(s_y, 1)

        @block.vector
        def _(dve):
            v = nc.vector
            chain = [0]

            def link(ins):
                chain[0] += 1
                ins.then_inc(s_dve, 1)
                dve.wait_ge(s_dve, chain[0])

            def tt(out, a, b, op=ALU.mult):
                return v.tensor_tensor(out=out, in0=a, in1=b, op=op)

            link(v.memset(xpad[:, :, 0:2], 0.0))
            v.memset(xpad[:, :, 2 + SEQ:4 + SEQ], 0.0).then_inc(s_pad0, 1)
            ps = wait_full(dve, "par")
            freed(v.tensor_copy(pcol, ps[:, 0:NPAR]), "par")
            wait_taken(dve, "par")
            for t in range(NT + 1):
                if t < NT:
                    dve.wait_ge(s_rstd, t + 1)
                    if t >= 2:
                        wait_full(dve, f"xT{t - 2}b")
                    v.tensor_scalar(out=xn[:, t % 2, :], in0=xsb[:, t, :], scalar1=rstd[:, t:t + 1], scalar2=None,
                                    op0=ALU.mult).then_inc(s_xn, 1)
                if t:
                    for h in range(2):
                        u = f"xT{t - 1}{'ab'[h]}"
                        ps = wait_full(dve, u)
                        freed(tt(hTm[:, 4 * h:4 * h + 4, (t - 1) * P:t * P], cut(ps[:, :], 4, P),
                                 over(pc_mix[:, 4 * h:4 * h + 4], P)), u)
            for b, u in zip(bias3, ("bg", "bu", "bd")):
                ps = wait_full(dve, u)
                freed(v.tensor_copy(b, ps[:, 0:NE * KT]), u)
            dve.wait_ge(s_rows, 16 * 6)
            v.tensor_copy(cut(gains[:, 0:AW], NH, HD), times(qk[:, 0:HD], NH))
            v.tensor_copy(cut(gains[:, AW:AW + KVW], NKV, HD), times(qk[:, HD:2 * HD], NKV)).then_inc(s_qss, 1)
            ps = wait_full(dve, "dt")
            freed(tt(dtr, cut(ps[:, 0:NT * 16], NT, 16), times(dtb, NT), ALU.add), "dt")
            wait_taken(dve, "dt")
            v.scalar_tensor_tensor(out=dta, in0=dtr, scalar=-1.0, in1=dtr, op0=ALU.mult,
                                   op1=ALU.max).then_inc(s_dta, 1)
            dve.wait_ge(s_dtl, 1)
            link(v.scalar_tensor_tensor(out=dtv, in0=dtr, scalar=0.0, in1=dta, op0=ALU.max, op1=ALU.add))
            v.scalar_tensor_tensor(out=da, in0=dtv, scalar=-1.0, in1=times(alog, NT), op0=ALU.mult,
                                   op1=ALU.mult).then_inc(s_da, 1)
            def silu(n):
                dve.wait_ge(s_sgx, n + 1)
                tt(xc[:, CHANNELS[n], :], xc[:, CHANNELS[n], :], sgx[n % 2]).then_inc(s_xc, 1)

            for n, ch in enumerate(CHANNELS):
                wait_taken(dve, f"xb{ch}")
                acc = xc[:, ch, :]
                link(v.tensor_scalar(out=acc, in0=xpad[:, n % 2, 0:SEQ], scalar1=pc_cw[:, ch:ch + 1],
                                     scalar2=pc_cb[:, ch:ch + 1], op0=ALU.mult, op1=ALU.add))
                for j in range(1, CONV):
                    ins = v.scalar_tensor_tensor(out=acc, in0=xpad[:, n % 2, j:j + SEQ],
                                                 scalar=pc_cw[:, j * CT + ch:j * CT + ch + 1],
                                                 in1=acc, op0=ALU.mult, op1=ALU.add)
                    if j < CONV - 1:
                        link(ins)
                ins.then_inc(s_conv, 1)
                if n:
                    silu(n - 1)
                else:
                    dve.wait_ge(s_conv, 1)
            silu(CT - 1)

            def rotate(t):
                dve.wait_ge(s_qsq, t + 1)
                v.tensor_reduce(out=qss, in_=cut(qk2, 10, HD), axis=AX.X, op=ALU.add).then_inc(s_qss, 1)
                dve.wait_ge(s_qrs, t + 1)
                link(tt(cut(qk, 10, HD), cut(qk, 10, HD), over(qrs, HD)))
                link(tt(qk, qk, gains))
                link(tt(cut(qk2, 10, HD), cut(qk, 10, HD), times(cos_t[:, t, :], 10)))
                if t:
                    wait_full(dve, f"tk{t - 1}")
                for axis in range(2):
                    for x in range(2):
                        o = axis * 32 + x * 16
                        i_ = axis * 32 + (1 - x) * 16
                        ins = tt(cut(qk3, 10, HD)[:, :, o:o + 16], cut(qk, 10, HD)[:, :, i_:i_ + 16],
                                 times(sin_t[:, t, o:o + 16], 10))
                link(ins)
                k3, k2 = (cut(b[:, AW:QKW], NKV, HD).unsqueeze(2).to_broadcast([P, NKV, 2, HD]) for b in (qk3, qk2))
                v.tensor_tensor(out=kd, in0=k3, in1=k2, op=ALU.add)
                tt(qk3[:, 0:AW], qk3[:, 0:AW], qk2[:, 0:AW], ALU.add).then_inc(s_rot, 1)

            def by_head(ap):
                return cut(ap, SH, HD)

            seg = [0]

            def chunk(c):
                if c:
                    dve.wait_ge(s_g, 4 * c)
                ps = wait_full(dve, f"cb{c}")
                tt(cut(cbm[:, 0, :], SG, P), cut(ps[:, 0:SG * P], SG, P), times(c_le, SG))
                freed(tt(cut(cbm[:, 1, :], SG, P), cut(ps[:, 0:SG * P], SG, P), times(c_ge, SG)), f"cb{c}")
                wait_taken(dve, f"tx{c}")
                if c:
                    wait_full(dve, f"{'sf' if c == 1 else 'sb'}{c - 1}")
                else:
                    wait_taken(dve, f"cs{NT - 1}")
                link(tt(by_head(xdtf), by_head(xs[:, c, :]), over(dtv[:, c, 0:SH], HD)))
                link(tt(by_head(xdtb), by_head(xs[:, c, :]), over(dtv[:, c, SH:2 * SH], HD)))
                tt(by_head(xwf), by_head(xdtf), over(ex[:, c, 16:24], HD))
                tt(by_head(xwb), by_head(xdtb), over(ex[:, c, 24:32], HD)).then_inc(s_xdt, 1)
                wait_taken(dve, f"cb{c}")
                for di in range(2):
                    for g in range(SG):
                        k = seg[0]
                        wait_taken(dve, f"sg{c}{'fb'[di]}{g}")
                        if c and k % 4 == 0:
                            wait_full(dve, f"yd{c - 1}")
                        tt(gdec[k % 4], eseg[k % 2], times(cbm[:, di, g * P:(g + 1) * P], HPG)).then_inc(s_g, 1)
                        seg[0] += 1

            def states(c):
                if c < NT - 1:
                    ps = wait_full(dve, f"sf{c}")
                    if c == 0:
                        wait_full(dve, f"z{NT - 1}")
                        freed(v.tensor_copy(prevf[1], ps[:, :]), "sf0")
                        wait_taken(dve, "sf0")
                    else:
                        link(tt(by_head(prevf[c + 1]), by_head(prevf[c]), over(ex[:, c, 32:40], HD)))
                        freed(tt(prevf[c + 1], ps[:, :], prevf[c + 1], ALU.add), f"sf{c}")
                        wait_taken(dve, f"sf{c}")
                if c:
                    ps = wait_full(dve, f"sb{c}")
                    freed(v.tensor_copy(prevb[c - 1], ps[:, :]), f"sb{c}")
                    wait_taken(dve, f"sb{c}")

            rotate(0)
            rotate(1)
            rotate(2)
            rotate(3)
            chunk(0)
            for c in range(NT):
                if c < NT - 1:
                    chunk(c + 1)
                states(c)
            link(tt(by_head(ytmp[0]), by_head(prevb[2]), over(ex[:, 2, 40:48], HD)))
            link(tt(prevb[1], prevb[1], ytmp[0], ALU.add))
            link(tt(by_head(ytmp[0]), by_head(prevb[1]), over(ex[:, 1, 40:48], HD)))
            tt(prevb[0], prevb[0], ytmp[0], ALU.add).then_inc(s_prev, 1)
            dve.wait_ge(s_prev, 1)

            def combine(i):
                dve.wait_ge(s_zsig, i + 1)
                link(tt(zs[:, i, :], zs[:, i, :], xc[:, i, :]))
                link(tt(by_head(ytmp[0]), by_head(xs[:, i, :]), over(dsk, HD)))
                link(tt(ytmp[0], ytmp[0], ydsb[:, i, :], ALU.add))
                for name, col, has in (("yf", 0, i > 0), ("yb", 8, i < NT - 1)):
                    if has:
                        ps = wait_full(dve, f"{name}{i}")
                        freed(tt(by_head(ytmp[1]), by_head(ps[:, :]), over(ex[:, i, col:col + 8], HD)), f"{name}{i}")
                        wait_taken(dve, f"{name}{i}")
                        link(tt(ytmp[0], ytmp[0], ytmp[1], ALU.add))
                if i:
                    wait_full(dve, f"tm{i - 1}b")
                else:
                    wait_full(dve, f"tk{NT - 1}")
                tt(mixs, ytmp[0], zs[:, i, :]).then_inc(s_ys, 1)

            for s in range(STEPS):
                if s < NPAIR:
                    if s >= 2:
                        wait_taken(dve, f"s{s - 2}b")
                    for h in range(2):
                        ps = wait_full(dve, f"s{s}{'ab'[h]}")
                        ins = v.reduce_max(nb[s % 2][:, h:h + 1], ps[:, :], AX.X)
                    link(ins)
                    v.tensor_scalar(out=nb[s % 2], in0=nb[s % 2], scalar1=-HD ** -0.5, scalar2=None,
                                    op0=ALU.mult).then_inc(s_nb, 1)
                if 1 <= s <= NPAIR:
                    n = s - 1
                    if n >= 2:
                        dve.wait_ge(s_of, n - 1)
                    ps = wait_full(dve, f"p{n}b")
                    freed(v.tensor_copy(probsT[n % 2 * 2 + 1], cut(ps[:, :], NT, P)), f"p{n}b")
                if turn_at(s, 6) is not None:
                    i = turn_at(s, 6)
                    dve.wait_ge(s_an, i + 1)
                    v.tensor_scalar(out=mixa, in0=mixa, scalar1=nrs[:, 0, i:i + 1], scalar2=None,
                                    op0=ALU.mult).then_inc(s_mixa, 1)
                if turn_at(s, 5) is not None:
                    i = turn_at(s, 5)
                    wait_taken(dve, f"s{4 * i + 3}b")
                    link(v.reciprocal(rsum, sums[:, i % 2, :]))
                    dve.wait_ge(s_of, 4 * i + 4)
                    if i:
                        wait_full(dve, f"tm{i - 1}b")
                    tt(cut(mixa, NH, HD), cut(bank[7][:, :], NH, HD), over(rsum, HD)).then_inc(s_ofree, 1)
                if turn_at(s, 3) is not None:
                    combine(turn_at(s, 3))
                if turn_at(s, 4) is not None:
                    i = turn_at(s, 4)
                    dve.wait_ge(s_yn, i + 1)
                    tt(cut(mixs, SG, GW), cut(mixs, SG, GW), over(nrs[:, 1, i * SG:(i + 1) * SG], GW)
                       ).then_inc(s_mixs, 1)
                if turn_at(s, TM) is not None:
                    t = turn_at(s, TM)
                    for h, gain in enumerate((pc_att, pc_ssm)):
                        u = f"tm{t}{'ab'[h]}"
                        ps = wait_full(dve, u)
                        freed(tt(hTm[:, 4 * h:4 * h + 4, t * P:(t + 1) * P], cut(ps[:, :], 4, P), over(gain, P)), u)
                if turn_at(s, OP) is not None:
                    t = turn_at(s, OP)
                    dve.wait_ge(s_xr[t], 16)
                    for h in range(2):
                        u = f"op{t}{'ab'[h]}"
                        ps = wait_full(dve, u)
                        part = x1[:, t, h * 512:h * 512 + 512]
                        freed(tt(part, ps[:, :], part, ALU.add), u)
                if turn_at(s, OP + 1) is not None:
                    t = turn_at(s, OP + 1)
                    dve.wait_ge(s_x1n, t + 1)
                    if t:
                        wait_full(dve, f"th{t - 1}b")
                        dve.wait_ge(s_hst, 16 * t)
                    else:
                        dve.wait_ge(s_gffn, 16)
                    v.scalar_tensor_tensor(out=hrw, in0=x1[:, t, :], scalar=nrs[:, 2, t:t + 1], in1=gffn,
                                           op0=ALU.mult, op1=ALU.mult).then_inc(s_h, 1)
                if turn_at(s, LG) is not None:
                    t = turn_at(s, LG)
                    ps = wait_full(dve, f"lg{t}")
                    freed(tt(lg[:, t, :], ps[:, 0:NE], brow, ALU.add), f"lg{t}")
                    wait_taken(dve, f"lg{t}")
                    link(v.max(m8[:, t, :], lg[:, t, :]))
                    link(v.max_index(ix8[:, t, :].bitcast(U32), m8[:, t, :], lg[:, t, :]))

            v.tensor_scalar(out=nmx, in0=m8[:, :, 0], scalar1=-1.0, scalar2=None, op0=ALU.mult).then_inc(s_rt, 1)
            link(v.tensor_copy(ixf, ix8.bitcast(U32)))
            iota_e = times(iota[:, 0:NE], NT)
            for k in range(TOPK):
                ins = tt(oh[k], iota_e, over(ixf[:, :, k], NE), ALU.is_equal)
            link(ins)
            link(tt(msk, oh[0], oh[1], ALU.add))
            link(tt(tmpr, oh[2], oh[3], ALU.add))
            tt(msk, msk, tmpr, ALU.add).then_inc(s_cnt, 1)
            dve.wait_ge(s_cnt, 1)
            dve.wait_ge(s_rte, NT)
            link(v.reciprocal(wrec, wsum))
            link(tt(ws, ws, over(wrec, TOPK)))
            for k in range(TOPK):
                link(tt(oh[k], oh[k], over(ws[:, :, k], NE)))
            link(tt(wgt, oh[0], oh[1], ALU.add))
            link(tt(tmpr, oh[2], oh[3], ALU.add))
            link(tt(payload[:, :, :, 1], wgt, tmpr, ALU.add))
            link(v.tensor_copy(payload[:, :, :, 0], over(tok_c, NE)))
            link(v.tensor_copy(payload[:, :, :, 2], times(ones[:, 0:NE], NT)))
            ps = wait_full(dve, "cum")
            link(v.tensor_copy(cnt, ps[:, NT * NE:NT * NE + NE]))
            pos = cut(ps[:, 0:NT * NE], NT, NE)
            freed(v.scalar_tensor_tensor(out=posm, in0=pos, scalar=1.0, in1=msk, op0=ALU.add, op1=ALU.mult), "cum")
            wait_taken(dve, "cum")
            link(v.tensor_scalar(out=posm, in0=posm, scalar1=-1.0, scalar2=None, op0=ALU.add))
            link(v.tensor_scalar(out=nch, in0=cnt, scalar1=float(P), scalar2=1.0, op0=ALU.is_gt, op1=ALU.add))
            for m in range(2, NT):
                link(v.scalar_tensor_tensor(out=nch, in0=cnt, scalar=float(m * P), in1=nch, op0=ALU.is_gt,
                                            op1=ALU.add))
            link(v.tensor_tensor_scan(out=cume, data0=ones[:, 0:NE], data1=nch, initial=0.0, op0=ALU.mult,
                                      op1=ALU.add))
            link(v.tensor_copy(cum_i.bitcast(I32), cume))
            link(tt(cums, cume, nch, ALU.subtract))
            link(v.tensor_scalar(out=ohi, in0=cume, scalar1=row_c, scalar2=None, op0=ALU.is_gt))
            link(v.scalar_tensor_tensor(out=ohi, in0=cums, scalar=row_c, in1=ohi, op0=ALU.is_le, op1=ALU.mult))
            link(v.scalar_tensor_tensor(out=are, in0=cums, scalar=float(P), in1=cnt, op0=ALU.mult, op1=ALU.add))
            link(v.scalar_tensor_tensor(out=itm, in0=ohi, scalar=1.0, in1=iota[:, 0:NE], op0=ALU.mult, op1=ALU.mult,
                                        accum_out=icol[:, 0:1]))
            link(v.scalar_tensor_tensor(out=itm, in0=ohi, scalar=1.0, in1=are, op0=ALU.mult, op1=ALU.mult,
                                        accum_out=icol[:, 1:2]))
            link(v.scalar_tensor_tensor(out=itm, in0=ohi, scalar=float(-P), in1=cums, op0=ALU.mult, op1=ALU.mult,
                                        accum_out=icol[:, 2:3]))
            link(v.scalar_tensor_tensor(out=icol[:, 1:2], in0=row_c, scalar=float(-P), in1=icol[:, 1:2],
                                        op0=ALU.mult, op1=ALU.add))
            link(v.scalar_tensor_tensor(out=icol[:, 2:3], in0=row_c, scalar=float(P), in1=icol[:, 2:3],
                                        op0=ALU.mult, op1=ALU.add))
            for n in range(3):
                ins = v.tensor_scalar(out=rhs3[:, n, :], in0=ident[:, 0:IW], scalar1=icol[:, n:n + 1], scalar2=None,
                                      op0=ALU.mult)
            ins.then_inc(s_tabr, 1)
            ps = wait_full(dve, "tab")
            link(v.tensor_copy(items_i.bitcast(I32), cut(ps[:, 0:3 * IW], 3, IW)[:, 0:2, :]))
            freed(v.tensor_copy(items_f, cut(ps[:, 0:3 * IW], 3, IW)), "tab")
            wait_taken(dve, "tab")
            v.memset(hrow, 0.0).then_inc(s_tab, 1)
            dve.wait_ge(s_tab, 1)

            def item_expert(i):
                return dve.value_load(items_i[0:1, 0, bass.ds(i, 1)].bitcast(I32), min_val=0, max_val=NE - 1)

            def rows_of(i):
                e = item_expert(i)
                for t in range(NT):
                    ins = v.tensor_scalar(out=onehot[:, t, :], in0=iota, scalar1=items_f[:, 2, bass.ds(i, 1)],
                                          scalar2=posm[:, t, bass.ds(e, 1)], op0=ALU.add, op1=ALU.is_equal)
                ins.then_inc(s_oh, 1)

            def indices():
                link(v.tensor_copy(dsp[:, 0:3], bank[4][:, 0:3]))
                link(v.scalar_tensor_tensor(out=tmp1, in0=dsp[:, 2:3], scalar=-FAR, in1=dsp[:, 0:1], op0=ALU.mult,
                                            op1=ALU.add))
                v.tensor_scalar(out=idx_g.bitcast(I32), in0=tmp1, scalar1=FAR, scalar2=None,
                                op0=ALU.add).then_inc(s_idx, 1)

            rows_of(0)
            dve.wait_ge(s_dsp, 1)
            indices()
            for credit in (s_gt, s_ut, s_at, s_yt):
                dve.sem_inc(credit, 1)
            nitems = dve.value_load(cum_i[0:1, NE - 1:NE].bitcast(I32), min_val=NE, max_val=MAX_ITEMS)
            with dve.Fori(0, MAX_ITEMS) as i:
                with dve.If(i < nitems):
                    e = item_expert(i)
                    for h in range(2):
                        bias = [over(b[:, bass.ds(e * KT + 4 * h, 4)], P) for b in bias3]
                        if h == 0:
                            dve.wait_ge(s_dsp, i + 1)
                            rows_of(i + 1)
                        dve.wait_ge(s_used[2 * h], i + 1)
                        tt(gb, cut(bank[0][:, :], 4, P), bias[0], ALU.add).then_inc(s_gt, 1)
                        dve.wait_ge(s_gt, 2 * i + h + 2)
                        v.tensor_scalar(out=gb, in0=gb, scalar1=LIMIT, scalar2=None, op0=ALU.min).then_inc(s_gb, 1)
                        dve.wait_ge(s_used[2 * h + 1], i + 1)
                        tt(ub, cut(bank[1][:, :], 4, P), bias[1], ALU.add).then_inc(s_ut, 1)
                        dve.wait_ge(s_ut, 2 * i + h + 2)
                        v.tensor_scalar(out=ub, in0=ub, scalar1=LIMIT, scalar2=-LIMIT, op0=ALU.min,
                                        op1=ALU.max).then_inc(s_uc, 1)
                        dve.wait_ge(s_uc, 2 * i + h + 1)
                        dve.wait_ge(s_gb, 2 * i + h + 1)
                        v.scalar_tensor_tensor(out=tb, in0=ub, scalar=1.0, in1=gb, op0=ALU.add,
                                               op1=ALU.mult).then_inc(s_tb, 1)
                        dve.wait_ge(s_tb, 2 * i + h + 1)
                        dve.wait_ge(s_sg, 2 * i + h + 1)
                        tt(actT[:, 4 * h:4 * h + 4, :], tb, sg).then_inc(s_at, 1)
                        if h == 0:
                            dve.wait_ge(s_landed, i + 1)
                            v.tensor_copy(idx_s.bitcast(I32), idx_g.bitcast(I32))
                            v.tensor_copy(w_s, dsp[:, 1:2]).then_inc(s_ws, 1)
                            dve.wait_ge(s_gath, 16 * i + 16)
                            dve.wait_ge(s_dsp, i + 2)
                            dve.wait_ge(s_ws, i + 1)
                            v.tensor_copy(dsp[:, 0:3], bank[4][:, 0:3]).then_inc(s_i1, 1)
                            dve.wait_ge(s_i1, i + 1)
                            v.scalar_tensor_tensor(out=tmp1, in0=dsp[:, 2:3], scalar=-FAR, in1=dsp[:, 0:1],
                                                   op0=ALU.mult, op1=ALU.add).then_inc(s_i2, 1)
                            dve.wait_ge(s_i2, i + 1)
                            v.tensor_scalar(out=idx_g.bitcast(I32), in0=tmp1, scalar1=FAR, scalar2=None,
                                            op0=ALU.add).then_inc(s_idx, 1)
                    dve.wait_ge(s_yf, i + 1)
                    for h, full in enumerate(s_used[4:6]):
                        dve.wait_ge(full, i + 1)
                        tt(yT[:, 4 * h:4 * h + 4, :], cut(bank[2 + h][:, :], 4, P),
                           over(bias3[2][:, bass.ds(e * KT + 4 * h, 4)], P), ALU.add).then_inc(s_yt, 1)

        @block.tensor
        def _(pe):
            T = nc.tensor

            def begin(u):
                turn, b = where[u]
                if turn:
                    pe.wait_ge(psum_free[b], turn)
                return bank[b]

            def end(ins, u):
                ins.then_inc(psum_full[where[u][1]], 1)

            def transposes(u, ins_):
                ps = begin(u)
                for n, a in enumerate(ins_):
                    k = a.shape[0]
                    last = T.transpose(ps[:, n * P:n * P + k], a, ident[0:k, 0:k])
                end(last, u)

            pe.wait_ge(s_const, 16)
            pe.wait_ge(s_par, 16 * 5)
            transposes("par", [praw[0:NPAR, :]])
            for t in range(NT):
                pe.wait_ge(s_xn, t + 1)
                for h in range(2):
                    transposes(f"xT{t}{'ab'[h]}", [xn[:, t % 2, k * P:(k + 1) * P] for k in range(4 * h, 4 * h + 4)])
            pe.wait_ge(s_bias, 16 * 3)
            for u, b in zip(("bg", "bu", "bd"), braw):
                transposes(u, [b[:, 0, :], b[:, 1, :]])
            for t in range(NT):
                wait_taken(pe, f"xT{t}b")
            pe.wait_ge(s_win[0], 16)
            ps = begin("dt")
            for t in range(NT):
                for k in range(KT):
                    last = T.matmul(ps[:, t * 16:(t + 1) * 16], hTm[:, k, t * P:(t + 1) * P], w_in[:, k, DT0:INW],
                                    start=(k == 0), stop=(k == KT - 1))
            end(last, "dt")
            for ch in CHANNELS:
                ps = begin(f"xb{ch}")
                for k in range(KT):
                    last = T.matmul(ps[:, :], w_in[:, k, XBC0 + ch * P:XBC0 + (ch + 1) * P], hTm[:, k, :],
                                    start=(k == 0), stop=(k == KT - 1))
                end(last, f"xb{ch}")

            def project(u, t, a, b, src=None, w=None):
                src, w = (hTm, w_in) if src is None else (src, w)
                ps = begin(u)
                for k in range(KT):
                    last = T.matmul(ps[:, 0:b - a], src[:, k, t * P:(t + 1) * P], w[:, k, a:b],
                                    start=(k == 0), stop=(k == KT - 1))
                end(last, u)

            def heads(t):
                pe.wait_ge(s_rot, t + 1)
                transposes(f"tq{t}", [qk3[:, n * P:(n + 1) * P] for n in range(4)])
                transposes(f"tk{t}", [kd[:, n, :, :].rearrange("p a b -> p (a b)") for n in range(NKV)])

            k_seg = [0]

            def decays(c):
                if c == NT:
                    return
                ps = begin(f"cb{c}")
                for g in range(SG):
                    last = T.matmul(ps[:, g * P:(g + 1) * P], xc[:, 4 + g, c * P:(c + 1) * P],
                                    xc[:, 6 + g, c * P:(c + 1) * P], start=True, stop=True)
                end(last, f"cb{c}")
                for di, upto in (("f", c_le), ("b", c_ge)):
                    for g in range(SG):
                        u, k = f"sg{c}{di}{g}", k_seg[0]
                        pe.wait_ge(s_sm, k + 1)
                        ps = begin(u)
                        for h in range(HPG):
                            last = T.matmul(ps[:, h * P:(h + 1) * P], sm[k % 2][:, h, :], upto, start=True, stop=True)
                        end(last, u)
                        k_seg[0] += 1

            pe.wait_ge(s_win[1], 16)
            for t in (0, 1):
                project(f"q{t}", t, 0, AW)
                project(f"kv{t}", t, AW, Z0)
            pe.wait_ge(s_da, 1)
            for c in range(NT):
                ps = begin(f"cs{c}")
                f, b = da[:, c, 0:SH], da[:, c, SH:2 * SH]
                for n, (m, r) in enumerate(((c_le, f), (c_ge, b), (c_gt, f), (c_lt, b))):
                    T.matmul(ps[:, n * 8:n * 8 + 8], m, r, start=True, stop=True)
                end(T.matmul(ps[:, 32:48], ones, da[:, c, :], start=True, stop=True), f"cs{c}")
            heads(0)
            pe.wait_ge(s_xc, CT)
            for c in range(NT):
                transposes(f"tx{c}", [xc[:, n, c * P:(c + 1) * P] for n in range(4)])
                transposes(f"tb{c}", [xc[:, 4 + n, c * P:(c + 1) * P] for n in range(SG)])
            project("q2", 2, 0, AW)
            project("kv2", 2, AW, Z0)
            heads(1)
            project("q3", 3, 0, AW)
            project("kv3", 3, AW, Z0)
            pe.wait_ge(s_win[2], 16)
            project("z0", 0, Z0, XBC0)
            project("z1", 1, Z0, XBC0)
            heads(2)
            decays(0)
            project("z2", 2, Z0, XBC0)
            project("z3", 3, Z0, XBC0)
            heads(3)
            for c in range(NT):
                decays(c + 1)
                wait_taken(pe, f"tb{c}")
                pe.wait_ge(s_xdt, c + 1)
                pe.wait_ge(s_g, 4 * c + 4)
                ps = begin(f"yd{c}")
                for h in range(SH):
                    g, hh = divmod(h, HPG)
                    o = slice(h * HD, (h + 1) * HD)
                    T.matmul(ps[:, o], gdec[g][:, hh, :], xdtf[:, o], start=True, stop=False)
                    last = T.matmul(ps[:, o], gdec[2 + g][:, hh, :], xdtb[:, o], start=False, stop=True)
                end(last, f"yd{c}")
                for name, w, has in (("sf", xwf, c < NT - 1), ("sb", xwb, c > 0)):
                    if has:
                        ps = begin(f"{name}{c}")
                        for g in range(SG):
                            last = T.matmul(ps[:, g * GW:(g + 1) * GW], brows[:, c, g * SN:(g + 1) * SN],
                                            w[:, g * GW:(g + 1) * GW], start=True, stop=True)
                        end(last, f"{name}{c}")

            def attend(p):
                i, j = divmod(p, 4)
                if i and j == 0:
                    pe.wait_ge(s_ofree, i)
                for h in range(2):
                    wait_taken(pe, f"p{p}{'ab'[h]}")
                for h in range(2):
                    head = 2 * j + h
                    kv = head // (NH // NKV)
                    for kt in range(NT):
                        last = T.matmul(bank[7][:, head * HD:(head + 1) * HD], probsT[p % 2 * 2 + h][:, kt, :],
                                        vs[:, kt, kv * HD:(kv + 1) * HD], start=(kt == 0), stop=(kt == NT - 1))
                last.then_inc(s_of, 1)

            for t in range(NT):
                wait_taken(pe, f"tk{t}")
            for s in range(STEPS):
                if s < NPAIR:
                    i, j = divmod(s, 4)
                    pss = [begin(f"s{s}{h}") for h in "ab"]
                    for h in range(2):
                        r = slice(h * HD, (h + 1) * HD)
                        end(T.matmul(pss[h][:, :], qT[r, j, i * P:(i + 1) * P], kT[r, 2 * j // (NH // NKV), :],
                                     start=True, stop=True), f"s{s}{'ab'[h]}")
                if 1 <= s <= NPAIR:
                    for h in range(2):
                        wait_taken(pe, f"s{s - 1}{'ab'[h]}")
                        transposes(f"p{s - 1}{'ab'[h]}",
                                   [probs[(s - 1) % 2 * 2 + h][:, n * P:(n + 1) * P] for n in range(NT)])
                if 2 <= s <= NPAIR + 1:
                    attend(s - 2)
                if turn_at(s, 3) is not None:
                    c = turn_at(s, 3)
                    pe.wait_ge(s_prev, 1)
                    for name, prev, has in (("yf", prevf, c > 0), ("yb", prevb, c < NT - 1)):
                        if has:
                            ps = begin(f"{name}{c}")
                            for g in range(SG):
                                last = T.matmul(ps[:, g * GW:(g + 1) * GW], xc[:, 6 + g, c * P:(c + 1) * P],
                                                prev[c][:, g * GW:(g + 1) * GW], start=True, stop=True)
                            end(last, f"{name}{c}")
                if turn_at(s, TM) is not None:
                    t = turn_at(s, TM)
                    pe.wait_ge(s_mixa, t + 1)
                    transposes(f"tm{t}a", [mixa[:, n * P:(n + 1) * P] for n in range(4)])
                    pe.wait_ge(s_mixs, t + 1)
                    transposes(f"tm{t}b", [mixs[:, n * P:(n + 1) * P] for n in range(4)])
                if turn_at(s, OP) is not None:
                    t = turn_at(s, OP)
                    wait_taken(pe, f"tm{t}a")
                    wait_taken(pe, f"tm{t}b")
                    pe.wait_ge(s_wout, 16)
                    for h in range(2):
                        project(f"op{t}{'ab'[h]}", t, h * 512, h * 512 + 512, hTm, w_out)
                if turn_at(s, TH) is not None:
                    t = turn_at(s, TH)
                    pe.wait_ge(s_h, t + 1)
                    for h in range(2):
                        transposes(f"th{t}{'ab'[h]}", [hrw[:, k * P:(k + 1) * P] for k in range(4 * h, 4 * h + 4)])
                if turn_at(s, LG) is not None:
                    t = turn_at(s, LG)
                    wait_taken(pe, f"th{t}a")
                    wait_taken(pe, f"th{t}b")
                    pe.wait_ge(s_wr, 16)
                    ps = begin(f"lg{t}")
                    for k in range(KT):
                        last = T.matmul(ps[:, 0:NE], hrT[:, k, :], wr[:, k, :], start=(k == 0), stop=(k == KT - 1))
                    end(last, f"lg{t}")
            pe.wait_ge(s_cnt, 1)
            ps = begin("cum")
            for t in range(NT + 1):
                o = ps[:, t * NE:(t + 1) * NE]
                for u in range(min(t, NT)):
                    last = T.matmul(o, ones, msk[:, u, :], start=(u == 0), stop=(t == NT and u == NT - 1))
                if t < NT:
                    T.matmul(o, c_lt, msk[:, t, :], start=(t == 0), stop=True)
            end(last, "cum")
            pe.wait_ge(s_tabr, 1)
            ps = begin("tab")
            end(T.matmul(ps[:, 0:3 * IW], ones, rhs3.rearrange("p a b -> p (a b)"), start=True, stop=True), "tab")

            for b in range(RINGB):
                turns = sum(1 for _, bb in where.values() if bb == b)
                pe.wait_ge(psum_free[b], turns)
            pe.wait_ge(s_tab, 1)

            def dispatch(i):
                e = pe.value_load(items_i[0:1, 0, bass.ds(i, 1)].bitcast(I32), min_val=0, max_val=NE - 1)
                for t in range(NT):
                    last = T.matmul(bank[4][:, 0:3], onehot[:, t, :], payload[:, t, bass.ds(e, 1), :].rearrange("p a b -> p (a b)"),
                                    start=(t == 0), stop=(t == NT - 1))
                last.then_inc(s_dsp, 1)

            def turn_rows():
                for k in range(KT):
                    last = T.transpose(bank[4 + k // 4][:, k % 4 * P:(k % 4 + 1) * P], hrow[:, k * P:(k + 1) * P], ident)
                last.then_inc(s_tin, 1)

            def products(i, ea):
                for s in range(4):
                    pe.wait_ge(s_full[s], 16 * ea + 16)
                    b, taken = (bank[0], s_gt) if s % 2 == 0 else (bank[1], s_ut)
                    pe.wait_ge(taken, 2 * i + s // 2 + 1)
                    for f in range(4):
                        for k in range(KT):
                            last = T.matmul(b[:, f * P:(f + 1) * P], slot[s][:, k, f * P:(f + 1) * P],
                                            hT[:, k, :], start=(k == 0), stop=(k == KT - 1))
                    last.then_inc(s_used[s], 1)
                    if s == 1:
                        pe.wait_ge(s_oh, i + 2)
                        dispatch(i + 1)
                for half in range(2):
                    pe.wait_ge(s_at, 2 * i + half + 2)
                    for m in range(2):
                        if half == 0:
                            pe.wait_ge(s_full[4 + m], 16 * ea + 16)
                            pe.wait_ge(s_yt, 2 * i + 1)
                        for f in range(4):
                            for k in range(4 * half, 4 * half + 4):
                                last = T.matmul(bank[2 + m][:, f * P:(f + 1) * P],
                                                slot[4 + m][:, k, f * P:(f + 1) * P], actT[:, k, :],
                                                start=(half == 0 and f == 0 and k == 0), stop=(k == KT - 1),
                                                skip_group_check=True)
                        if half:
                            last.then_inc(s_used[4 + m], 1)

            pe.wait_ge(s_oh, 1)
            dispatch(0)
            pe.wait_ge(s_gath, 16)
            turn_rows()
            pe.sem_inc(s_yf, 1)
            nitems = pe.value_load(cum_i[0:1, NE - 1:NE].bitcast(I32), min_val=NE, max_val=MAX_ITEMS)
            with pe.Fori(0, MAX_ITEMS) as i:
                with pe.If(i < nitems):
                    ea = pe.value_load(items_i[0:1, 0, bass.ds(i, 1)].bitcast(I32), min_val=0, max_val=NE - 1)
                    pe.wait_ge(s_hT, i + 1)
                    products(i, ea)
                    pe.wait_ge(s_gath, 16 * i + 32)
                    turn_rows()
                    pe.wait_ge(s_yt, 2 * i + 3)
                    pe.wait_ge(s_y, 2 * i + 1)
                    for k in range(KT):
                        last = T.transpose(bank[6 + k // 4][:, k % 4 * P:(k % 4 + 1) * P], yT[:, k, :], ident)
                    last.then_inc(s_yf, 1)


INPUTS = ["x", "norm_mix", "w_in", "q_norm", "k_norm", "conv_w", "conv_b", "dt_bias", "a_log", "d_skip",
          "ssm_norm", "attn_norm", "w_out", "norm_ffn", "w_router", "b_router", "w_gate", "b_gate",
          "w_up", "b_up", "w_down", "b_down"]


def kernel(**inputs):
    import concourse.bacc as bacc
    from concourse.bass_utils import run_bass_kernel_spmd

    nc = bacc.Bacc("TRN2", target_bir_lowering=False, num_devices=1)
    arrays, d = {}, {}
    for name in INPUTS:
        arrays[f"in_{name}"] = np.ascontiguousarray(inputs[name])
    arrays["in_const"] = constants()
    for name, a in arrays.items():
        d[name[3:]] = nc.dram_tensor(name, a.shape, mybir.dt.from_np(a.dtype), kind="ExternalInput").ap()
    out = nc.dram_tensor("out", (1, SEQ, DM), F32, kind="ExternalOutput").ap()
    hn = nc.dram_tensor("normed_rows", (SEQ, DM), F32, kind="Internal").ap()
    hybrid_layer(nc, d, out, hn)
    r = run_bass_kernel_spmd(nc, [arrays], core_ids=[0])
    return r.results[0]["out"]
```

```python
import concourse.bass as bass
from concourse import mybir
from contextlib import ExitStack
import numpy as np

F32 = mybir.dt.float32
F32R = mybir.dt.float32r
I32 = mybir.dt.int32
U32 = mybir.dt.uint32
ALU = mybir.AluOpType
ACT = mybir.ActivationFunctionType
AX = mybir.AxisListType

P = 128
SEQ, DM = 512, 1024
NT = SEQ // P
KT = DM // P
HD = 64
NH, NKV = 8, 2
SH, SG, SN = 8, 2, 128
HPG = SH // SG
AW = NH * HD
KVW = NKV * HD
SW = SH * HD
GW = SW // SG
XBC = SW + 2 * SG * SN
CONV = 5
Z0 = AW + 2 * KVW
XBC0 = Z0 + SW
DT0 = XBC0 + XBC
INW = DT0 + 2 * SH
CT = XBC // P
NE, TOPK = 32, 4
DE = DM
EPS = 1e-6
LIMIT, ALPHA = 7.0, 1.702
GRID_W = 64
IW = 52
ROWS = (64, 96, P)
PK = 2
PR = KT // PK
PW = PK * DE
SLOT = 4096
NRAW = 6
FIRST = 2 * PR
MAX_ITEMS = NE + SEQ * TOPK // P
GROUP = 8
FAR = 8192.0

C_LE, C_GE, C_GT, C_LT, C_ID, C_ONE, C_IOTA = (n * P for n in range(7))
C_COS = 7 * P
C_SIN = C_COS + NT * HD
C_EPS = C_SIN + NT * HD
C_ROW = C_EPS + 1
C_TOK = C_ROW + 1
C_SEL = C_TOK + NT
C_END = C_SEL + NE


def constants():
    f = np.float32
    t, q = np.arange(P)[:, None], np.arange(P)[None, :]
    c = np.zeros((P, C_END), f)
    for at, m in ((C_LE, t <= q), (C_GE, t >= q), (C_GT, t > q), (C_LT, t < q), (C_ID, t == q)):
        c[:, at:at + P] = m
    c[:, C_ONE:C_ONE + P] = 1
    c[:, C_IOTA:C_IOTA + P] = q
    half = HD // 2
    inv = (f(10000.0) ** (-np.arange(0, half, 2, dtype=f) / f(half))).astype(f)
    tok = np.arange(SEQ)
    ar = (tok // GRID_W).astype(f)[:, None] * inv
    ac = (tok % GRID_W).astype(f)[:, None] * inv
    cos = np.concatenate([np.cos(ar), np.cos(ar), np.cos(ac), np.cos(ac)], 1).astype(f)
    sin = np.concatenate([-np.sin(ar), np.sin(ar), -np.sin(ac), np.sin(ac)], 1).astype(f)
    c[:, C_COS:C_SIN] = cos.reshape(NT, P, HD).transpose(1, 0, 2).reshape(P, -1)
    c[:, C_SIN:C_EPS] = sin.reshape(NT, P, HD).transpose(1, 0, 2).reshape(P, -1)
    c[:, C_EPS] = EPS
    c[:, C_ROW] = np.arange(P)
    c[:2 * NE, C_SEL:C_END] = np.tile(np.eye(NE, dtype=f), (2, 1))
    c[:, C_TOK:C_SEL] = np.arange(P)[:, None] + P * np.arange(NT)
    return c


def units():
    u = ["par"] + [f"xT{t}{h}" for t in range(NT) for h in "ab"] + ["dt"]
    u += [f"xb{ch}" for ch in CHANNELS]
    u += ["q0", "kv0", "q1", "kv1"] + [f"cs{c}" for c in range(NT)] + ["tq0", "tk0"]
    for c in range(NT):
        u += [f"tx{c}", f"tb{c}"]
    u += ["q2", "kv2", "tq1", "tk1", "q3", "kv3", "z0", "tq2", "tk2"] + decay_units(0)
    u += ["z1", "z2", "z3", "tq3", "tk3"]
    for c in range(NT):
        u += decay_units(c + 1) + [f"yd{c}"] + [f"sf{c}"] * (c < NT - 1) + [f"sb{c}"] * (c > 0)
    for s in range(STEPS):
        if s < NPAIR:
            u += [f"s{s}a", f"s{s}b"]
        if 1 <= s <= NPAIR:
            u += [f"p{s - 1}a", f"p{s - 1}b"]
        if s % 4 == 3 and s < NPAIR:
            u += [f"yf{s // 4}"] * (s // 4 > 0) + [f"yb{s // 4}"] * (s // 4 < NT - 1)
        for first, name, parts in ((TM, "tm", "ab"), (OP, "op", "ab"), (TH, "th", "ab"), (LG, "lg", " ")):
            if turn_at(s, first) is not None:
                u += [f"{name}{turn_at(s, first)}{h}".strip() for h in parts]
    return u + ["cum", "tab"]


def decay_units(c):
    return [f"cb{c}"] + [f"sg{c}{d}{g}" for d in "fb" for g in range(SG)] if c < NT else []


CHANNELS = (6, 7, 4, 5, 0, 1, 2, 3)
NPAIR = NT * NH // 2
TM, OP, TH, LG = 7, 8, 10, 11
STEPS = LG + 4 * (NT - 1) + 1


def turn_at(s, first):
    t, r = divmod(s - first, 4)
    return t if r == 0 and 0 <= t < NT else None


def hybrid_layer(nc, d, out, hn):
    ctx = ExitStack()
    with ctx:
        def sem(name):
            return ctx.enter_context(nc.semaphore(name))

        with nc.sbuf_tensor("mixer_ring", [P, 6 * SLOT], F32) as ring, \
                nc.sbuf_tensor("mixer_rows", [P, 2 * SLOT], F32) as rows:
            pass
        raw_a = ctx.enter_context(nc.sbuf_tensor("raw_pieces", [P, 2 * SLOT], F32))
        hi_t = ctx.enter_context(nc.sbuf_tensor("hi_pieces", [P, 2 * SLOT], F32R))
        lo_t = ctx.enter_context(nc.sbuf_tensor("lo_pieces", [P, 2 * SLOT], F32R))
        part = ctx.enter_context(nc.sbuf_tensor("part_rows", [P, 2 * SLOT], F32R))
        REST = 20400
        rest = ctx.enter_context(nc.sbuf_tensor("rest", [P, REST], F32))
        at = [0]

        def take(n):
            at[0] += n
            assert at[0] <= REST, at[0]
            return rest[:, at[0] - n:at[0]]

        def cut(ap, *sizes):
            names = "abcd"[:len(sizes)]
            return ap.rearrange(f"p ({' '.join(names)}) -> p {' '.join(names)}", **dict(zip(names, sizes)))

        const = take(C_END)
        c_le, c_ge, c_gt, c_lt, ident, ones, iota = (const[:, n * P:(n + 1) * P] for n in range(7))
        cos_t = cut(const[:, C_COS:C_SIN], NT, HD)
        sin_t = cut(const[:, C_SIN:C_EPS], NT, HD)
        eps_c, row_c, tok_c = const[:, C_EPS:C_EPS + 1], const[:, C_ROW:C_ROW + 1], const[:, C_TOK:C_SEL]
        one_c, sel_c = ones[:, 0:1], const[:, C_SEL:C_END]
        dtb, alog, dsk = take(2 * SH), take(2 * SH), take(SH)
        gains = take((NH + NKV) * HD)
        brow = take(NE)
        NPAR = 8 + 8 + CONV * CT + 4 + 4
        pcol = take(NPAR)
        pc_mix, pc_cb, pc_cw = pcol[:, 0:8], pcol[:, 8:16], pcol[:, 16:16 + CONV * CT]
        pc_att, pc_ssm = pcol[:, 56:60], pcol[:, 60:64]
        hTm = cut(rows[:, 0:SLOT], KT, SEQ)
        xsb_w = rows[:, SLOT:2 * SLOT]
        xsb = cut(xsb_w, NT, DM)
        sm = [cut(xsb_w[:, n * 512:n * 512 + 512], HPG, P) for n in range(2)]
        eseg = [cut(xsb_w[:, 1024 + n * 512:1536 + n * 512], HPG, P) for n in range(2)]
        gdec = [[cut(w[:, n * 512:n * 512 + 512], HPG, P) for n in range(4)]
                for w in (xsb_w[:, 2048:4096], rows[:, 2048:4096])]
        probs = [xsb_w[:, n * 512:n * 512 + 512] for n in range(4)]
        probsT = [cut(xsb_w[:, 2048 + n * 512:2560 + n * 512], NT, P) for n in range(4)]
        xc_w = take(CT * SEQ)
        xc = cut(xc_w, CT, SEQ)
        zs_w = take(NT * SW)
        zs = cut(zs_w, NT, SW)
        vs_w = take(NT * KVW)
        vs = cut(vs_w, NT, KVW)
        payload = cut(vs_w[:, 0:NT * NE * 3], NT, NE, 3)
        posm = cut(vs_w[:, NT * NE * 3:NT * NE * 4], NT, NE)
        qT_w = take(NH // 2 * SEQ)
        qT = cut(qT_w, NH // 2, SEQ)
        kT = cut(take(NKV * SEQ), NKV, SEQ)
        xs_w = take(NT * SW)
        xs = cut(xs_w, NT, SW)
        br_w = take(NT * SG * SN)
        brows = cut(br_w, NT, SG * SN)
        gffn = br_w
        xpad_w = take(2 * (SEQ + CONV - 1))
        xpad = cut(xpad_w, 2, SEQ + CONV - 1)
        ytmp = [xpad_w[:, n * 512:n * 512 + 512] for n in range(2)]
        QKW = (NH + NKV) * HD
        qk_w = take(3 * QKW + 2 * KVW)
        qk, qk2, qk3 = (qk_w[:, n * QKW:(n + 1) * QKW] for n in range(3))
        kd = cut(qk_w[:, 3 * QKW:], NKV, 2, HD)
        mixa, mixs, junk = (qk_w[:, n * 512:n * 512 + 512] for n in range(3))
        ssq = take(NT); rstd = take(NT)
        dtr = cut(take(NT * 16), NT, 16); dta = cut(take(NT * 16), NT, 16)
        dtv = cut(take(NT * 16), NT, 16); da = cut(take(NT * 16), NT, 16)
        ex = cut(take(NT * 48), NT, 48)
        qss = take(10); qrs = take(10)
        nb = [take(2) for _ in range(2)]
        sums = cut(take(2 * NH), 2, NH); rsum = take(NH)
        nss = cut(take(3 * 8), 3, 8); nrs = cut(take(3 * 8), 3, 8)
        lg = cut(take(NT * NE), NT, NE)
        m8 = cut(take(NT * 8), NT, 8); ix8 = cut(take(NT * 8), NT, 8); ixf = cut(take(NT * 8), NT, 8)
        nmx = take(NT); ws = cut(take(NT * TOPK), NT, TOPK); wsum = take(NT); wrec = take(NT)
        items_f = cut(take(3 * IW), 3, IW)
        left_i = take(IW)
        expert_i = take(IW)
        steady_i = take(1)
        idx_tab, w_tab = take(IW), take(IW)
        dsp = take(4); tmp1 = take(1); idx_g = take(1); idx_s = take(1)
        gb, ub, sg = (xc_w[:, n * DM:(n + 1) * DM] for n in range(3))
        hrow = xc_w[:, 3 * DM:4 * DM]
        bstage = xc_w[0:2 * NE, 0:3 * DM]
        yrow = qT_w[:, 0:DM]
        onehot = cut(qT_w[:, DM:DM + NT * P], NT, P)
        raw = [cut(w, PK, DE) for w in (*(raw_a[:, n * PW:(n + 1) * PW] for n in range(4)), xs_w, zs_w)]
        hi, lo = ([cut(t[:, n * PW:(n + 1) * PW], PK, DE) for n in range(PR)] for t in (hi_t, lo_t))
        hTh, hTl, aTh, aTl = (part[:, n * DM:(n + 1) * DM] for n in range(4))
        btab = part[:, 4 * DM:7 * DM]
        sel_gu, sel_d = part[:, 7 * DM:7 * DM + P], part[:, 7 * DM + P:7 * DM + 2 * P]
        rt = qT_w.rearrange("p (a b) -> p a b", b=P)
        oh = [cut(rt[:, n, :], NT, NE) for n in range(4)]
        msk, wgt, tmpr = (cut(rt[:, n, :], NT, NE) for n in (4, 5, 6))
        cnt, nch, cume, cums, ohi, are = (rt[:, 7 + n // 4, n % 4 * NE:(n % 4 + 1) * NE] for n in range(6))
        icol = rt[:, 9, 0:4]
        rhs3 = cut(rt[:, 14:16, :].rearrange("p a b -> p (a b)")[:, 0:3 * IW], 3, IW)
        itm = rt[:, 12, 0:32]
        tmpp = cut(rt[:, 13, :], NT, NE)
        offs = cut(rt[:, 11, :], NT, NE)
        w_in = cut(ring[:, 0:KT * INW], KT, INW)
        x1 = cut(ring[:, SLOT:2 * SLOT], NT, DM)
        prev_w = ring[:, 2 * SLOT:2 * SLOT + 3072]
        prevf = {c: prev_w[:, (c - 1) * 512:c * 512] for c in (1, 2, 3)}
        prevb = {c: prev_w[:, 1536 + c * 512:2048 + c * 512] for c in (0, 1, 2)}
        ydsb = cut(ring[:, 2 * SLOT + 3072:2 * SLOT + 5120], NT, SW)
        w_out = cut(ring[:, 13312:21504], KT, DM)
        ta = ring[:, 21504:23552]
        xn = cut(ta, 2, DM)
        xd = [[w[:, n * 512:n * 512 + 512] for n in range(4)] for w in (ta, rows[:, 0:2048])]
        hrw = ta[:, 0:DM]
        hrT = cut(ta[:, DM:2 * DM], KT, P)
        sgx = [ring[:, 23552 + n * 512:24064 + n * 512] for n in range(2)]
        cbm = cut(ring[:, 23552:24064], 2, SG * P)
        wr = cut(ring[:, 24064:24064 + KT * NE], KT, NE)
        praw = hTm[:, 0, 0:P]
        junkx = qT.rearrange("p a b -> p (a b)")[:, 0:DM]

        pair = [ctx.enter_context(nc.psum_tensor(f"pair{n}", [P, 1024], F32)) for n in range(4)]
        bank = [pair[n // 2][:, n % 2 * 512:n % 2 * 512 + 512] for n in range(8)]
        gate_ps, up_ps, down_ps, turn_ps = pair
        RINGB = 7
        order = units()
        where = {u: divmod(n, RINGB) for n, u in enumerate(order)}
        assert len(where) == len(order)
        psum_full = [sem(f"psum_full{n}") for n in range(RINGB)]
        psum_free = [sem(f"psum_free{n}") for n in range(RINGB)]

        def wait_full(eng, u):
            turn, b = where[u]
            eng.wait_ge(psum_full[b], turn + 1)
            return bank[b]

        def freed(ins, u):
            ins.then_inc(psum_free[where[u][1]], 1)

        def wait_taken(eng, u):
            turn, b = where[u]
            eng.wait_ge(psum_free[b], turn + 1)

        s_const, s_par, s_rows = sem("const_in"), sem("par_in"), sem("rows_in")
        s_x = [sem(f"x{t}_in") for t in range(NT)]
        s_win = [sem(f"w_in{n}_in") for n in range(3)]
        s_wout, s_wr, s_gffn = sem("w_out_in"), sem("w_router_in"), sem("gain_ffn_in")
        s_xr = [sem(f"x{t}_again") for t in range(NT)]
        s_rstd, s_xn, s_pad0 = sem("rstd_ready"), sem("xn_ready"), sem("pads_zeroed")
        s_act, s_dve = sem("act_chain"), sem("dve_chain")
        s_conv, s_sgx, s_xc = sem("conv_ready"), sem("conv_sigmoid"), sem("xc_ready")
        s_dta, s_dtl, s_da = sem("dt_abs"), sem("dt_log"), sem("da_ready")
        s_sm, s_g = sem("scaled_mask"), sem("decay_ready")
        s_xdt, s_prev = sem("xdt_ready"), sem("prev_ready")
        s_qss, s_qrs, s_rot = sem("qk_copied"), sem("qk_rstd"), sem("qk_rotated")
        s_qsq = sem("qk_squares")
        s_zsig = sem("z_sigmoid")
        s_nb = sem("row_max")
        s_of, s_ofree = sem("attn_full"), sem("attn_taken")
        s_ys, s_yn = sem("ssd_rows"), sem("ssd_rstd")
        s_an = sem("attn_rstd")
        s_mixa, s_mixs = sem("mix_attn"), sem("mix_ssd")
        s_x1n, s_h = sem("x1_rstd"), sem("h_ready")
        s_hst, s_ost = sem("h_stored"), sem("x1_stored")
        s_rt, s_rte, s_tabr, s_cnt = sem("logit_max"), sem("weights_exp"), sem("table_cols"), sem("mask_ready")
        s_tab, s_wts, s_pay = sem("tables_ready"), sem("weights_ready"), sem("payload_ready")
        s_raw = [sem(f"raw{n}_in") for n in range(NRAW)]
        s_hi = [sem(f"hi{n}_ready") for n in range(PR)]
        s_lo = [sem(f"lo{n}_ready") for n in range(PR)]
        s_used = [sem(f"piece{n}_used") for n in range(PR)]
        s_bst, s_bhi, s_btab = sem("biases_in"), sem("biases_rounded"), sem("bias_table")
        s_selgu, s_seld = sem("expert_selected"), sem("expert_selected_down")
        s_oh, s_dsp, s_dt, s_i1, s_idx = (sem("onehot_ready"), sem("dispatch_full"), sem("dispatch_taken"),
                                          sem("index_part"), sem("index_ready"))
        s_ig, s_is, s_gath, s_scat = sem("gather_index"), sem("scatter_index"), sem("gathered"), sem("scattered")
        s_landed, s_moves, s_zero = sem("additions_landed"), sem("row_moves_begun"), sem("rows_zeroed")
        s_gf, s_gb, s_sg = sem("gate_full"), sem("gate_clamped"), sem("gate_sigmoid")
        s_uf, s_u1, s_u2, s_acted = sem("up_full"), sem("up_clamped"), sem("gate_up"), sem("act_ready")
        s_af, s_ah, s_al = sem("act_turned"), sem("act_hi"), sem("act_lo")
        s_hf, s_hh, s_hl = sem("rows_turned"), sem("rows_hi"), sem("rows_lo")
        s_df, s_y = sem("down_full"), sem("y_ready")

        w_in_d = d["w_in"][0].rearrange("(k p) n -> p k n", p=P)
        w_out_d = d["w_out"][0].rearrange("(k p) n -> p k n", p=P)
        x_d = d["x"][0].rearrange("(t p) n -> t p n", p=P)
        out_d = out[0]
        hn_d = hn

        def bc(row, n=P):
            return row.partition_broadcast(n)

        def over(ap, k):
            return ap.unsqueeze(2).to_broadcast([P, ap.shape[1], k])

        def times(ap, k):
            return ap.unsqueeze(1).to_broadcast([P, k, ap.shape[1]])

        WEIGHTS = ("w_gate", "w_up", "w_down")

        def piece_source(m, e, r):
            return d[WEIGHTS[m]][0, e].rearrange("(k p) n -> p k n", p=P)[:, r * PK:(r + 1) * PK, :]

        def turn(q, b):
            return 3 * q + (b // PR + 1)

        def raw_turn(q, b):
            return 2 * q + (b // NRAW + 1)

        def at_least(eng, sem_, n):
            if not (isinstance(n, int) and n <= 0):
                eng.wait_ge(sem_, n)

        def item_expert(eng, i):
            return eng.value_load(expert_i[0:1, bass.ds(i, 1)].bitcast(I32), min_val=0, max_val=NE - 1)

        def steady_turns(eng):
            return eng.value_load(steady_i[0:1, 0:1].bitcast(I32), min_val=NE - 2, max_val=MAX_ITEMS)

        block = ctx.enter_context(nc.Block())

        @block.sync
        def _(sp):
            def load(q, b, m, e):
                if not (isinstance(q, int) and 12 * q + b < NRAW):
                    old = b - NRAW
                    sp.wait_ge(s_lo[old % PR], turn(q, old))
                sp.dma_start(raw[b % NRAW], piece_source(m, e, b % PR)).then_inc(s_raw[b % NRAW], 16)

            sp.dma_start(const, d["const"]).then_inc(s_const, 16)
            for t in range(NT):
                sp.dma_start(xsb[:, t, :], x_d[t]).then_inc(s_x[t], 16)
            for name, r0, n in (("norm_mix", 0, 8), ("conv_b", 8, 8), ("conv_w", 16, 40),
                                ("attn_norm", 56, 4), ("ssm_norm", 60, 4)):
                src = d[name][0]
                if name == "conv_w":
                    src = src.rearrange("k (c p) -> (k c) p", p=P)
                else:
                    src = src.rearrange("(c p) -> c p", p=P)
                sp.dma_start(praw[r0:r0 + n, :], src).then_inc(s_par, 16)
            for n, (a, b) in enumerate(((XBC0, INW), (0, Z0), (Z0, XBC0))):
                sp.dma_start(w_in[:, :, a:b], w_in_d[:, :, a:b]).then_inc(s_win[n], 16)
                if n == 0:
                    for dst, src in ((dtb, d["dt_bias"][0].rearrange("a h -> (a h)")),
                                     (alog, d["a_log"][0].rearrange("a h -> (a h)")),
                                     (dsk, d["d_skip"][0]), (brow, d["b_router"][0]),
                                     (qk[:, 0:HD], d["q_norm"][0]), (qk[:, HD:2 * HD], d["k_norm"][0])):
                        sp.dma_start(dst, bc(src)).then_inc(s_rows, 16)
            wait_full(sp, f"z{NT - 1}")
            for t in range(NT):
                sp.dma_start(x1[:, t, :], x_d[t]).then_inc(s_xr[t], 16)
            sp.dma_start(w_out, w_out_d).then_inc(s_wout, 16)
            sp.dma_start(wr, d["w_router"][0].rearrange("(k p) n -> p k n", p=P)).then_inc(s_wr, 16)
            load(0, 0, 0, 0)
            load(0, 1, 0, 0)
            wait_full(sp, f"sb{NT - 1}")
            sp.dma_start(gffn, bc(d["norm_ffn"][0])).then_inc(s_gffn, 16)
            for t in range(NT):
                if t == NT - 1:
                    sp.wait_ge(s_ys, NT)
                    wait_full(sp, f"yf{NT - 1}")
                    for b in (4, 5):
                        load(0, b, 1, 0)
                    for n, name in enumerate(("b_gate", "b_up", "b_down")):
                        for h in range(2):
                            sp.dma_start(bstage[h * NE:(h + 1) * NE, n * DM:(n + 1) * DM],
                                         d[name][0]).then_inc(s_bst, 16)
                wait_taken(sp, f"op{t}a")
                wait_taken(sp, f"op{t}b")
                sp.dma_start(out_d[t * P:(t + 1) * P, :], x1[:, t, :]).then_inc(s_ost, 16)
                sp.wait_ge(s_h, t + 1)
                sp.dma_start(hn_d[t * P:(t + 1) * P, :], hrw).then_inc(s_hst, 16)
            sp.wait_ge(s_ost, 16 * NT)
            for b in (2, 3):
                load(0, b, 0, 0)
            for b in (6, 7):
                load(0, b, 1, 0)
            sp.wait_ge(s_tab, 1)

            def loads(q):
                for m, i in ((0, q + 2), (1, q + 2), (2, q + 1)):
                    e = item_expert(sp, i)
                    for r in range(PR):
                        load(q, FIRST + 12 + m * PR + r, m, e)

            loads(-1)
            steady = steady_turns(sp)
            with sp.Fori(0, MAX_ITEMS // GROUP) as group:
                with sp.If(group * GROUP < steady):
                    with sp.Fori(0, GROUP) as n:
                        q = group * GROUP + n
                        with sp.If(q < steady):
                            loads(q)
            e = item_expert(sp, steady + 1)
            for r in range(PR):
                load(steady, FIRST + 12 + r, 2, e)

        @block.gpsimd
        def _(pool):
            k = 0
            pool.wait_ge(s_da, 1)
            pool.wait_ge(s_const, 16)
            for c in range(NT):
                for di, mask in enumerate((c_gt, c_lt)):
                    for g in range(SG):
                        if k >= 2:
                            n = k - 2
                            wait_full(pool, f"sg{n // 4}{'fb'[n // 2 % 2]}{n % 2}")
                        elif k == 0:
                            wait_full(pool, f"xT{NT - 1}b")
                        nc.gpsimd.tensor_tensor(
                            out=sm[k % 2], in0=times(mask, HPG),
                            in1=over(da[:, c, di * SH + g * HPG:di * SH + (g + 1) * HPG], P),
                            op=ALU.mult).then_inc(s_sm, 1)
                        k += 1
            wait_full(pool, f"yf{NT - 1}")
            pool.wait_ge(s_ys, NT)
            nc.gpsimd.memset(hrow, 0.0).then_inc(s_zero, 1)
            pool.wait_ge(s_zero, 1)
            pool.wait_ge(s_of, NPAIR)
            nc.gpsimd.memset(btab[2 * NE:P, :].bitcast(F32), 0.0).then_inc(s_zero, 1)
            pool.wait_ge(s_zero, 2)
            pool.wait_ge(s_bhi, 1)
            nc.gpsimd.tensor_tensor(out=btab[NE:2 * NE, :], in0=bstage[NE:2 * NE, :], in1=btab[NE:2 * NE, :],
                                    op=ALU.subtract).then_inc(s_btab, 1)
            pool.wait_ge(s_btab, 1)
            small = [0]

            def link(ins):
                small[0] += 1
                ins.then_inc(s_pay, 1)
                pool.wait_ge(s_pay, small[0])

            p = nc.gpsimd
            link(p.tensor_copy(payload[:, :, :, 0], over(tok_c, NE)))
            link(p.tensor_copy(payload[:, :, :, 2], times(ones[:, 0:NE], NT)))
            pool.wait_ge(s_wts, 1)
            for k in range(TOPK):
                link(p.tensor_tensor(out=oh[k], in0=oh[k], in1=over(ws[:, :, k], NE), op=ALU.mult))
            link(p.tensor_tensor(out=wgt, in0=oh[0], in1=oh[1], op=ALU.add))
            link(p.tensor_tensor(out=tmpp, in0=oh[2], in1=oh[3], op=ALU.add))
            link(p.tensor_tensor(out=payload[:, :, :, 1], in0=wgt, in1=tmpp, op=ALU.add))

            def split(q, b):
                r = b % PR
                pool.wait_ge(s_hi[r], turn(q, b))
                nc.gpsimd.tensor_tensor(out=lo[r], in0=raw[b % NRAW], in1=hi[r], op=ALU.subtract).then_inc(s_lo[r], 1)

            split(0, 0)
            split(0, 1)
            pool.wait_ge(s_hst, 16 * NT)
            pool.wait_ge(s_ost, 16 * NT)
            pool.wait_ge(s_tab, 1)

            def by_count(i, move):
                left = pool.value_load(left_i[0:1, bass.ds(i, 1)].bitcast(I32), min_val=0, max_val=SEQ)

                def choose(sizes):
                    if len(sizes) == 1:
                        move(sizes[0])
                        return
                    with pool.If(left < sizes[0] + 1):
                        move(sizes[0])
                    with pool.Else():
                        choose(sizes[1:])

                choose(ROWS)

            def gather(i):
                pool.wait_ge(s_idx, i + 1)
                at_least(pool, s_gath, 16 * i)
                at_least(pool, s_hf, i)
                pool.sem_inc(s_moves, 1)
                nc.gpsimd.tensor_copy(idx_g.bitcast(I32), idx_tab[:, bass.ds(i, 1)].bitcast(I32)).then_inc(s_ig, 1)
                pool.wait_ge(s_ig, i + 1)
                pool.sem_inc(s_moves, 1)

                def move(n):
                    nc.gpsimd.indirect_dma_start(
                        out=hrow[0:n, :], out_offset=None, in_=hn_d,
                        in_offset=bass.IndirectOffsetOnAxis(ap=idx_g[0:n, :].bitcast(I32), axis=0),
                        bounds_check=SEQ - 1, oob_is_err=False).then_inc(s_gath, 16)

                by_count(i, move)

            def scatter(i):
                pool.wait_ge(s_y, i + 1)
                pool.sem_inc(s_moves, 1)
                nc.gpsimd.tensor_copy(idx_s.bitcast(I32), idx_tab[:, bass.ds(i, 1)].bitcast(I32)).then_inc(s_is, 1)
                pool.wait_ge(s_is, i + 1)
                pool.sem_inc(s_moves, 1)

                def move(n):
                    nc.gpsimd.indirect_dma_start(
                        out=out_d, out_offset=bass.IndirectOffsetOnAxis(ap=idx_s[0:n, :].bitcast(I32), axis=0),
                        in_=yrow[0:n, :], in_offset=None, bounds_check=SEQ - 1, oob_is_err=False,
                        compute_op=ALU.add).then_inc(s_scat, 16)

                by_count(i, move)

            def landed(i):
                pool.wait_ge(s_scat, 16 * i + 16)
                pool.sem_inc(s_landed, 1)

            pool.wait_ge(s_btab, 1)
            gather(0)
            pool.sem_inc(s_landed, 1)
            split(0, PR - 1)
            gather(1)
            split(0, 2 * PR - 1)
            gather(2)

            def steps(q):
                split(q, FIRST + 12 + PR - 1)
                if not isinstance(q, int):
                    scatter(q)
                split(q, FIRST + 12 + 2 * PR - 1)
                if not isinstance(q, int):
                    landed(q)
                split(q, FIRST + 12 + 3 * PR - 1)
                gather(q + 4)

            steps(-1)
            steady = steady_turns(pool)
            with pool.Fori(0, MAX_ITEMS // GROUP) as group:
                with pool.If(group * GROUP < steady):
                    with pool.Fori(0, GROUP) as n:
                        q = group * GROUP + n
                        with pool.If(q < steady):
                            steps(q)
            scatter(steady)
            landed(steady)
            scatter(steady + 1)
            landed(steady + 1)
            pool.wait_ge(s_gath, 16 * steady + 64)

        @block.scalar
        def _(act):
            chain = [0]

            def link(ins):
                chain[0] += 1
                ins.then_inc(s_act, 1)
                act.wait_ge(s_act, chain[0])

            def rms(out, ss, n):
                link(nc.scalar.activation(out, ss, ACT.Ln, scale=1.0 / n, bias=eps_c))
                return nc.scalar.activation(out, out, ACT.Exp, scale=-0.5)

            act.wait_ge(s_const, 16)
            for t in range(NT):
                act.wait_ge(s_x[t], 16)
                link(nc.scalar.activation(junkx, xsb[:, t, :], ACT.Square, accum_out=ssq[:, t:t + 1]))
            rms(rstd, ssq, DM).then_inc(s_rstd, 1)
            act.wait_ge(s_rows, 16 * 6)
            link(nc.scalar.activation(alog, alog, ACT.Exp))
            act.wait_ge(s_dta, 1)
            link(nc.scalar.activation(dta, dta, ACT.Exp, scale=-1.0))
            nc.scalar.activation(dta, dta, ACT.Ln, bias=one_c).then_inc(s_dtl, 1)
            act.wait_ge(s_pad0, 1)
            def conv_sigmoid(n):
                act.wait_ge(s_conv, n + 1)
                if n >= 2:
                    act.wait_ge(s_xc, n - 1)
                nc.scalar.activation(sgx[n % 2], xc[:, CHANNELS[n], :], ACT.Sigmoid).then_inc(s_sgx, 1)

            for n, ch in enumerate(CHANNELS):
                if n >= 2:
                    act.wait_ge(s_conv, n - 1)
                ps = wait_full(act, f"xb{ch}")
                freed(nc.scalar.activation(xpad[:, n % 2, 2:2 + SEQ], ps[:, :], ACT.Copy), f"xb{ch}")
                if n:
                    conv_sigmoid(n - 1)
            conv_sigmoid(CT - 1)

            def copy_out(u, dst, n=512):
                ps = wait_full(act, u)
                src = ps[:, 0:n]
                if len(dst.shape) == 3:
                    src = cut(src, dst.shape[1], dst.shape[2])
                freed(nc.scalar.activation(dst, src, ACT.Copy), u)

            def take_qkv(t):
                act.wait_ge(s_qss, 1)
                if t:
                    act.wait_ge(s_rot, t)
                copy_out(f"q{t}", qk[:, 0:AW])
                ps = wait_full(act, f"kv{t}")
                link(nc.scalar.activation(qk[:, AW:QKW], ps[:, 0:KVW], ACT.Copy))
                freed(nc.scalar.activation(vs[:, t, :], ps[:, KVW:2 * KVW], ACT.Copy), f"kv{t}")
                wait_taken(act, f"q{t}")
                nc.scalar.activation(qk2, qk, ACT.Square).then_inc(s_qsq, 1)
                act.wait_ge(s_qss, t + 2)
                rms(qrs, qss, HD).then_inc(s_qrs, 1)

            def take_heads(t):
                copy_out(f"tq{t}", qT[:, :, t * P:(t + 1) * P])
                copy_out(f"tk{t}", kT[:, :, t * P:(t + 1) * P], NKV * P)

            seg = [0]

            def decays(c):
                if c == NT:
                    return
                for di in "fb":
                    for g in range(SG):
                        k = seg[0]
                        if k >= 2:
                            act.wait_ge(s_g, k - 1)
                        elif k == 0:
                            wait_full(act, f"xT{NT - 1}b")
                        unit = f"sg{c}{di}{g}"
                        ps = wait_full(act, unit)
                        freed(nc.scalar.activation(eseg[k % 2], cut(ps[:, :], HPG, P), ACT.Exp), unit)
                        seg[0] += 1

            take_qkv(0)
            take_qkv(1)
            for c in range(NT):
                ps = wait_full(act, f"cs{c}")
                freed(nc.scalar.activation(ex[:, c, :], ps[:, 0:48], ACT.Exp), f"cs{c}")
            take_heads(0)
            for c in range(NT):
                copy_out(f"tx{c}", xs[:, c, :])
                copy_out(f"tb{c}", brows[:, c, :], SG * SN)
            take_qkv(2)
            take_heads(1)
            take_qkv(3)
            copy_out("z0", zs[:, 0, :])
            take_heads(2)
            decays(0)
            copy_out("z1", zs[:, 1, :])
            copy_out("z2", zs[:, 2, :])
            copy_out("z3", zs[:, 3, :])
            take_heads(3)
            for c in range(NT):
                decays(c + 1)
                copy_out(f"yd{c}", ydsb[:, c, :])
            for c in range(NT):
                nc.scalar.activation(xc[:, c, :], zs[:, c, :], ACT.Sigmoid).then_inc(s_zsig, 1)

            for s in range(STEPS):
                if s < NPAIR:
                    act.wait_ge(s_nb, s + 1)
                    if s >= 2:
                        wait_full(act, f"p{s - 2}b")
                    for h in range(2):
                        ps = wait_full(act, f"s{s}{'ab'[h]}")
                        head = s % 4 * 2 + h
                        freed(nc.scalar.activation(probs[s % 2 * 2 + h], ps[:, :], ACT.Exp, scale=HD ** -0.5,
                                                   bias=nb[s % 2][:, h:h + 1],
                                                   accum_out=sums[:, s // 4 % 2, head:head + 1]), f"s{s}{'ab'[h]}")
                if 1 <= s <= NPAIR:
                    n = s - 1
                    if n >= 2:
                        act.wait_ge(s_of, n - 1)
                    ps = wait_full(act, f"p{n}a")
                    freed(nc.scalar.activation(probsT[n % 2 * 2], cut(ps[:, :], NT, P), ACT.Copy), f"p{n}a")
                if turn_at(s, 5) is not None:
                    i = turn_at(s, 5)
                    act.wait_ge(s_ofree, i + 1)
                    link(nc.scalar.activation(junk, mixa, ACT.Square, accum_out=nss[:, 0, i:i + 1]))
                    rms(nrs[:, 0, i:i + 1], nss[:, 0, i:i + 1], AW).then_inc(s_an, 1)
                if s == NPAIR + 3:
                    act.wait_ge(s_bst, 16 * 6)
                    act.wait_ge(s_of, NPAIR)
                    nc.scalar.activation(btab[0:2 * NE, :], bstage, ACT.Copy).then_inc(s_bhi, 1)
                if turn_at(s, 3) is not None:
                    i = turn_at(s, 3)
                    act.wait_ge(s_ys, i + 1)
                    for g in range(SG):
                        col = i * SG + g
                        link(nc.scalar.activation(junk[:, 0:GW], mixs[:, g * GW:(g + 1) * GW], ACT.Square,
                                                  accum_out=nss[:, 1, col:col + 1]))
                    rms(nrs[:, 1, i * SG:(i + 1) * SG], nss[:, 1, i * SG:(i + 1) * SG], GW).then_inc(s_yn, 1)
                if turn_at(s, OP) is not None:
                    t = turn_at(s, OP)
                    wait_taken(act, f"op{t}a")
                    wait_taken(act, f"op{t}b")
                    if t:
                        wait_full(act, f"lg{t - 1}")
                    else:
                        wait_full(act, f"sb{NT - 1}")
                    link(nc.scalar.activation(hrT.rearrange("p a b -> p (a b)"), x1[:, t, :], ACT.Square,
                                              accum_out=nss[:, 2, t:t + 1]))
                    rms(nrs[:, 2, t:t + 1], nss[:, 2, t:t + 1], DM).then_inc(s_x1n, 1)
                if turn_at(s, TH) is not None:
                    t = turn_at(s, TH)
                    for h in range(2):
                        copy_out(f"th{t}{'ab'[h]}", hrT[:, 4 * h:4 * h + 4, :])
            def split(q, b):
                r = b % PR
                act.wait_ge(s_raw[b % NRAW], 16 * raw_turn(q, b))
                at_least(act, s_used[r], turn(q, b - PR))
                nc.scalar.activation(hi[r], raw[b % NRAW], ACT.Copy).then_inc(s_hi[r], 1)

            split(0, 0)
            split(0, 1)
            act.wait_ge(s_rt, 1)
            for t in range(NT):
                nc_w = nc.scalar.activation(ws[:, t, :], m8[:, t, 0:TOPK], ACT.Exp, bias=nmx[:, t:t + 1],
                                            accum_out=wsum[:, t:t + 1])
                nc_w.then_inc(s_rte, 1)

            def splits(q, m):
                for r in range(PR):
                    split(q, m * PR + r)

            def take_rows(i):
                act.wait_ge(s_hf, i + 1)
                nc.scalar.activation(hTh, turn_ps[:, :], ACT.Copy).then_inc(s_hh, 1)

            def sigmoid(i):
                act.wait_ge(s_gb, i + 1)
                at_least(act, s_acted, i)
                nc.scalar.activation(sg, gb, ACT.Sigmoid, scale=ALPHA).then_inc(s_sg, 1)

            def take_act(i):
                act.wait_ge(s_af, i + 1)
                at_least(act, s_df, i)
                nc.scalar.activation(aTh, turn_ps[:, :], ACT.Copy).then_inc(s_ah, 1)

            split(0, 2)
            split(0, 3)
            take_rows(0)
            splits(0, 1)
            sigmoid(0)

            def steps(q):
                splits(q, 5)
                if isinstance(q, int):
                    take_rows(1)
                splits(q, 6)
                take_act(q + 1)
                sigmoid(q + 2)
                splits(q, 7)
                take_rows(q + 3)

            steps(-1)
            steady = steady_turns(act)
            with act.Fori(0, MAX_ITEMS // GROUP) as group:
                with act.If(group * GROUP < steady):
                    with act.Fori(0, GROUP) as n:
                        q = group * GROUP + n
                        with act.If(q < steady):
                            steps(q)
            for r in range(PR - 1):
                split(steady, FIRST + 12 + r)
            take_act(steady + 1)
            split(steady, FIRST + 12 + PR - 1)

        @block.vector
        def _(dve):
            v = nc.vector
            chain = [0]

            def link(ins):
                chain[0] += 1
                ins.then_inc(s_dve, 1)
                dve.wait_ge(s_dve, chain[0])

            def tt(out, a, b, op=ALU.mult):
                return v.tensor_tensor(out=out, in0=a, in1=b, op=op)

            link(v.memset(xpad[:, :, 0:2], 0.0))
            v.memset(xpad[:, :, 2 + SEQ:4 + SEQ], 0.0).then_inc(s_pad0, 1)
            ps = wait_full(dve, "par")
            freed(v.tensor_copy(pcol, ps[:, 0:NPAR]), "par")
            wait_taken(dve, "par")
            for t in range(NT + 1):
                if t < NT:
                    dve.wait_ge(s_rstd, 1)
                    if t >= 2:
                        wait_full(dve, f"xT{t - 2}b")
                    v.tensor_scalar(out=xn[:, t % 2, :], in0=xsb[:, t, :], scalar1=rstd[:, t:t + 1], scalar2=None,
                                    op0=ALU.mult).then_inc(s_xn, 1)
                if t:
                    for h in range(2):
                        u = f"xT{t - 1}{'ab'[h]}"
                        ps = wait_full(dve, u)
                        freed(tt(hTm[:, 4 * h:4 * h + 4, (t - 1) * P:t * P], cut(ps[:, :], 4, P),
                                 over(pc_mix[:, 4 * h:4 * h + 4], P)), u)
            dve.wait_ge(s_rows, 16 * 6)
            v.tensor_copy(cut(gains[:, 0:AW], NH, HD), times(qk[:, 0:HD], NH))
            v.tensor_copy(cut(gains[:, AW:AW + KVW], NKV, HD), times(qk[:, HD:2 * HD], NKV)).then_inc(s_qss, 1)
            ps = wait_full(dve, "dt")
            freed(tt(dtr, cut(ps[:, 0:NT * 16], NT, 16), times(dtb, NT), ALU.add), "dt")
            wait_taken(dve, "dt")
            v.scalar_tensor_tensor(out=dta, in0=dtr, scalar=-1.0, in1=dtr, op0=ALU.mult,
                                   op1=ALU.max).then_inc(s_dta, 1)
            dve.wait_ge(s_dtl, 1)
            link(v.scalar_tensor_tensor(out=dtv, in0=dtr, scalar=0.0, in1=dta, op0=ALU.max, op1=ALU.add))
            v.scalar_tensor_tensor(out=da, in0=dtv, scalar=-1.0, in1=times(alog, NT), op0=ALU.mult,
                                   op1=ALU.mult).then_inc(s_da, 1)
            def silu(n):
                dve.wait_ge(s_sgx, n + 1)
                tt(xc[:, CHANNELS[n], :], xc[:, CHANNELS[n], :], sgx[n % 2]).then_inc(s_xc, 1)

            for n, ch in enumerate(CHANNELS):
                wait_taken(dve, f"xb{ch}")
                acc = xc[:, ch, :]
                link(v.tensor_scalar(out=acc, in0=xpad[:, n % 2, 0:SEQ], scalar1=pc_cw[:, ch:ch + 1],
                                     scalar2=pc_cb[:, ch:ch + 1], op0=ALU.mult, op1=ALU.add))
                for j in range(1, CONV):
                    ins = v.scalar_tensor_tensor(out=acc, in0=xpad[:, n % 2, j:j + SEQ],
                                                 scalar=pc_cw[:, j * CT + ch:j * CT + ch + 1],
                                                 in1=acc, op0=ALU.mult, op1=ALU.add)
                    if j < CONV - 1:
                        link(ins)
                ins.then_inc(s_conv, 1)
                if n:
                    silu(n - 1)
                else:
                    dve.wait_ge(s_conv, 1)
            silu(CT - 1)

            def rotate(t):
                dve.wait_ge(s_qsq, t + 1)
                v.tensor_reduce(out=qss, in_=cut(qk2, 10, HD), axis=AX.X, op=ALU.add).then_inc(s_qss, 1)
                dve.wait_ge(s_qrs, t + 1)
                link(tt(cut(qk, 10, HD), cut(qk, 10, HD), over(qrs, HD)))
                link(tt(qk, qk, gains))
                link(tt(cut(qk2, 10, HD), cut(qk, 10, HD), times(cos_t[:, t, :], 10)))
                if t:
                    wait_full(dve, f"tk{t - 1}")
                for axis in range(2):
                    for x in range(2):
                        o = axis * 32 + x * 16
                        i_ = axis * 32 + (1 - x) * 16
                        ins = tt(cut(qk3, 10, HD)[:, :, o:o + 16], cut(qk, 10, HD)[:, :, i_:i_ + 16],
                                 times(sin_t[:, t, o:o + 16], 10))
                link(ins)
                k3, k2 = (cut(b[:, AW:QKW], NKV, HD).unsqueeze(2).to_broadcast([P, NKV, 2, HD]) for b in (qk3, qk2))
                v.tensor_tensor(out=kd, in0=k3, in1=k2, op=ALU.add)
                tt(qk3[:, 0:AW], qk3[:, 0:AW], qk2[:, 0:AW], ALU.add).then_inc(s_rot, 1)

            def by_head(ap):
                return cut(ap, SH, HD)

            seg = [0]

            def chunk(c):
                if c:
                    dve.wait_ge(s_g, 4 * c)
                ps = wait_full(dve, f"cb{c}")
                tt(cut(cbm[:, 0, :], SG, P), cut(ps[:, 0:SG * P], SG, P), times(c_le, SG))
                freed(tt(cut(cbm[:, 1, :], SG, P), cut(ps[:, 0:SG * P], SG, P), times(c_ge, SG)), f"cb{c}")
                wait_taken(dve, f"tx{c}")
                if c == 1:
                    wait_full(dve, f"z{NT - 1}")
                elif c >= 2:
                    wait_full(dve, f"{'sf' if c == 2 else 'sb'}{c - 2}")
                else:
                    wait_taken(dve, f"cs{NT - 1}")
                xdtf, xdtb, xwf, xwb = xd[c % 2]
                link(tt(by_head(xdtf), by_head(xs[:, c, :]), over(dtv[:, c, 0:SH], HD)))
                link(tt(by_head(xdtb), by_head(xs[:, c, :]), over(dtv[:, c, SH:2 * SH], HD)))
                tt(by_head(xwf), by_head(xdtf), over(ex[:, c, 16:24], HD))
                tt(by_head(xwb), by_head(xdtb), over(ex[:, c, 24:32], HD)).then_inc(s_xdt, 1)
                wait_taken(dve, f"cb{c}")
                for di in range(2):
                    for g in range(SG):
                        k = seg[0]
                        wait_taken(dve, f"sg{c}{'fb'[di]}{g}")
                        if c >= 2 and k % 4 == 0:
                            wait_full(dve, f"yd{c - 2}")
                        tt(gdec[c % 2][k % 4], eseg[k % 2], times(cbm[:, di, g * P:(g + 1) * P], HPG)).then_inc(s_g, 1)
                        seg[0] += 1

            def states(c):
                if c < NT - 1:
                    ps = wait_full(dve, f"sf{c}")
                    if c == 0:
                        wait_full(dve, f"z{NT - 1}")
                        freed(v.tensor_copy(prevf[1], ps[:, :]), "sf0")
                        wait_taken(dve, "sf0")
                    else:
                        link(tt(by_head(prevf[c + 1]), by_head(prevf[c]), over(ex[:, c, 32:40], HD)))
                        freed(tt(prevf[c + 1], ps[:, :], prevf[c + 1], ALU.add), f"sf{c}")
                        wait_taken(dve, f"sf{c}")
                if c:
                    ps = wait_full(dve, f"sb{c}")
                    freed(v.tensor_copy(prevb[c - 1], ps[:, :]), f"sb{c}")
                    wait_taken(dve, f"sb{c}")

            rotate(0)
            rotate(1)
            rotate(2)
            rotate(3)
            chunk(0)
            for c in range(NT):
                if c < NT - 1:
                    chunk(c + 1)
                states(c)
            link(tt(by_head(ytmp[0]), by_head(prevb[2]), over(ex[:, 2, 40:48], HD)))
            link(tt(prevb[1], prevb[1], ytmp[0], ALU.add))
            link(tt(by_head(ytmp[0]), by_head(prevb[1]), over(ex[:, 1, 40:48], HD)))
            tt(prevb[0], prevb[0], ytmp[0], ALU.add).then_inc(s_prev, 1)
            dve.wait_ge(s_prev, 1)

            def combine(i):
                dve.wait_ge(s_zsig, i + 1)
                link(tt(zs[:, i, :], zs[:, i, :], xc[:, i, :]))
                link(tt(by_head(ytmp[0]), by_head(xs[:, i, :]), over(dsk, HD)))
                link(tt(ytmp[0], ytmp[0], ydsb[:, i, :], ALU.add))
                for name, col, has in (("yf", 0, i > 0), ("yb", 8, i < NT - 1)):
                    if has:
                        ps = wait_full(dve, f"{name}{i}")
                        freed(tt(by_head(ytmp[1]), by_head(ps[:, :]), over(ex[:, i, col:col + 8], HD)), f"{name}{i}")
                        wait_taken(dve, f"{name}{i}")
                        link(tt(ytmp[0], ytmp[0], ytmp[1], ALU.add))
                if i:
                    wait_full(dve, f"tm{i - 1}b")
                else:
                    wait_full(dve, f"tk{NT - 1}")
                tt(mixs, ytmp[0], zs[:, i, :]).then_inc(s_ys, 1)

            for s in range(STEPS):
                if s < NPAIR:
                    if s >= 2:
                        wait_taken(dve, f"s{s - 2}b")
                    for h in range(2):
                        ps = wait_full(dve, f"s{s}{'ab'[h]}")
                        ins = v.reduce_max(nb[s % 2][:, h:h + 1], ps[:, :], AX.X)
                    link(ins)
                    v.tensor_scalar(out=nb[s % 2], in0=nb[s % 2], scalar1=-HD ** -0.5, scalar2=None,
                                    op0=ALU.mult).then_inc(s_nb, 1)
                if 1 <= s <= NPAIR:
                    n = s - 1
                    if n >= 2:
                        dve.wait_ge(s_of, n - 1)
                    ps = wait_full(dve, f"p{n}b")
                    freed(v.tensor_copy(probsT[n % 2 * 2 + 1], cut(ps[:, :], NT, P)), f"p{n}b")
                if turn_at(s, 6) is not None:
                    i = turn_at(s, 6)
                    dve.wait_ge(s_an, i + 1)
                    v.tensor_scalar(out=mixa, in0=mixa, scalar1=nrs[:, 0, i:i + 1], scalar2=None,
                                    op0=ALU.mult).then_inc(s_mixa, 1)
                if turn_at(s, 5) is not None:
                    i = turn_at(s, 5)
                    wait_taken(dve, f"s{4 * i + 3}b")
                    link(v.reciprocal(rsum, sums[:, i % 2, :]))
                    dve.wait_ge(s_of, 4 * i + 4)
                    if i:
                        wait_full(dve, f"tm{i - 1}b")
                    tt(cut(mixa, NH, HD), cut(bank[7][:, :], NH, HD), over(rsum, HD)).then_inc(s_ofree, 1)
                if turn_at(s, 3) is not None:
                    combine(turn_at(s, 3))
                if turn_at(s, 4) is not None:
                    i = turn_at(s, 4)
                    dve.wait_ge(s_yn, i + 1)
                    tt(cut(mixs, SG, GW), cut(mixs, SG, GW), over(nrs[:, 1, i * SG:(i + 1) * SG], GW)
                       ).then_inc(s_mixs, 1)
                if turn_at(s, TM) is not None:
                    t = turn_at(s, TM)
                    for h, gain in enumerate((pc_att, pc_ssm)):
                        u = f"tm{t}{'ab'[h]}"
                        ps = wait_full(dve, u)
                        freed(tt(hTm[:, 4 * h:4 * h + 4, t * P:(t + 1) * P], cut(ps[:, :], 4, P), over(gain, P)), u)
                if turn_at(s, OP) is not None:
                    t = turn_at(s, OP)
                    dve.wait_ge(s_xr[t], 16)
                    for h in range(2):
                        u = f"op{t}{'ab'[h]}"
                        ps = wait_full(dve, u)
                        part = x1[:, t, h * 512:h * 512 + 512]
                        freed(tt(part, ps[:, :], part, ALU.add), u)
                if turn_at(s, OP + 1) is not None:
                    t = turn_at(s, OP + 1)
                    dve.wait_ge(s_x1n, t + 1)
                    if t:
                        wait_full(dve, f"th{t - 1}b")
                        dve.wait_ge(s_hst, 16 * t)
                    else:
                        dve.wait_ge(s_gffn, 16)
                    v.scalar_tensor_tensor(out=hrw, in0=x1[:, t, :], scalar=nrs[:, 2, t:t + 1], in1=gffn,
                                           op0=ALU.mult, op1=ALU.mult).then_inc(s_h, 1)
                if turn_at(s, LG) is not None:
                    t = turn_at(s, LG)
                    ps = wait_full(dve, f"lg{t}")
                    freed(tt(lg[:, t, :], ps[:, 0:NE], brow, ALU.add), f"lg{t}")
                    wait_taken(dve, f"lg{t}")
                    link(v.max(m8[:, t, :], lg[:, t, :]))
                    link(v.max_index(ix8[:, t, :].bitcast(U32), m8[:, t, :], lg[:, t, :]))

            v.tensor_scalar(out=nmx, in0=m8[:, :, 0], scalar1=-1.0, scalar2=None, op0=ALU.mult).then_inc(s_rt, 1)
            link(v.tensor_copy(ixf, ix8.bitcast(U32)))
            iota_e = times(iota[:, 0:NE], NT)
            for k in range(TOPK):
                ins = tt(oh[k], iota_e, over(ixf[:, :, k], NE), ALU.is_equal)
            link(ins)
            link(tt(msk, oh[0], oh[1], ALU.add))
            link(tt(tmpr, oh[2], oh[3], ALU.add))
            tt(msk, msk, tmpr, ALU.add).then_inc(s_cnt, 1)
            dve.wait_ge(s_cnt, 1)
            dve.wait_ge(s_rte, NT)
            link(v.reciprocal(wrec, wsum))
            tt(ws, ws, over(wrec, TOPK)).then_inc(s_wts, 1)
            def split(q, b):
                r = b % PR
                dve.wait_ge(s_hi[r], turn(q, b))
                tt(lo[r], raw[b % NRAW], hi[r], ALU.subtract).then_inc(s_lo[r], 1)

            ps = wait_full(dve, "cum")
            total = cut(ps[:, NT * NE:2 * NT * NE], NT, NE)
            link(v.memset(offs[:, 0, :], 0.0))
            for t in range(NT):
                link(tt(offs[:, t + 1, :] if t < NT - 1 else cnt, total[:, t, :], offs[:, t, :], ALU.add))
            link(tt(offs, cut(ps[:, 0:NT * NE], NT, NE), offs, ALU.add))
            freed(v.scalar_tensor_tensor(out=posm, in0=offs, scalar=1.0, in1=msk, op0=ALU.add, op1=ALU.mult), "cum")
            wait_taken(dve, "cum")
            link(v.tensor_scalar(out=posm, in0=posm, scalar1=-1.0, scalar2=None, op0=ALU.add))
            link(v.tensor_scalar(out=nch, in0=cnt, scalar1=float(P), scalar2=1.0, op0=ALU.is_gt, op1=ALU.add))
            for m in range(2, NT):
                link(v.scalar_tensor_tensor(out=nch, in0=cnt, scalar=float(m * P), in1=nch, op0=ALU.is_gt,
                                            op1=ALU.add))
            link(v.tensor_tensor_scan(out=cume, data0=ones[:, 0:NE], data1=nch, initial=0.0, op0=ALU.mult,
                                      op1=ALU.add))
            link(v.tensor_scalar(out=steady_i.bitcast(I32), in0=cume[:, NE - 1:NE], scalar1=-2.0, scalar2=None,
                                 op0=ALU.add))
            link(tt(cums, cume, nch, ALU.subtract))
            link(v.tensor_scalar(out=ohi, in0=cume, scalar1=row_c, scalar2=None, op0=ALU.is_gt))
            link(v.scalar_tensor_tensor(out=ohi, in0=cums, scalar=row_c, in1=ohi, op0=ALU.is_le, op1=ALU.mult))
            link(v.scalar_tensor_tensor(out=itm, in0=ohi, scalar=1.0, in1=iota[:, 0:NE], op0=ALU.mult, op1=ALU.mult,
                                        accum_out=icol[:, 0:1]))
            link(v.scalar_tensor_tensor(out=itm, in0=ohi, scalar=float(-P), in1=cums, op0=ALU.mult, op1=ALU.mult,
                                        accum_out=icol[:, 1:2]))
            link(v.scalar_tensor_tensor(out=icol[:, 1:2], in0=row_c, scalar=float(P), in1=icol[:, 1:2],
                                        op0=ALU.mult, op1=ALU.add))
            link(v.scalar_tensor_tensor(out=are, in0=cums, scalar=float(P), in1=cnt, op0=ALU.mult, op1=ALU.add))
            link(v.scalar_tensor_tensor(out=itm, in0=ohi, scalar=1.0, in1=are, op0=ALU.mult, op1=ALU.mult,
                                        accum_out=icol[:, 2:3]))
            link(v.scalar_tensor_tensor(out=icol[:, 2:3], in0=row_c, scalar=float(-P), in1=icol[:, 2:3],
                                        op0=ALU.mult, op1=ALU.add))
            link(v.tensor_scalar(out=icol[:, 2:3], in0=icol[:, 2:3], scalar1=0.0, scalar2=None, op0=ALU.max))
            for n in range(3):
                ins = v.tensor_scalar(out=rhs3[:, n, :], in0=ident[:, 0:IW], scalar1=icol[:, n:n + 1], scalar2=None,
                                      op0=ALU.mult)
            ins.then_inc(s_tabr, 1)
            ps = wait_full(dve, "tab")
            freed(v.tensor_copy(items_f, cut(ps[:, 0:3 * IW], 3, IW)), "tab")
            wait_taken(dve, "tab")
            link(v.tensor_copy(left_i.bitcast(I32), items_f[:, 2, :]))
            v.tensor_copy(expert_i.bitcast(I32), items_f[:, 0, :]).then_inc(s_tab, 1)
            dve.wait_ge(s_tab, 1)

            def rows_of(i):
                at_least(dve, s_dsp, i)
                e = item_expert(dve, i)
                for t in range(NT):
                    ins = v.tensor_scalar(out=onehot[:, t, :], in0=iota, scalar1=items_f[:, 1, bass.ds(i, 1)],
                                          scalar2=posm[:, t, bass.ds(e, 1)], op0=ALU.add, op1=ALU.is_equal)
                ins.then_inc(s_oh, 1)

            def indices(i):
                dve.wait_ge(s_dsp, i + 1)
                at_least(dve, s_idx, i)
                v.tensor_copy(dsp[:, 0:3], down_ps[:, 0:3]).then_inc(s_dt, 1)
                dve.wait_ge(s_dt, i + 1)
                v.tensor_scalar(out=w_tab[:, bass.ds(i, 1)], in0=dsp[:, 1:2], scalar1=1.0, scalar2=None, op0=ALU.mult)
                v.scalar_tensor_tensor(out=tmp1, in0=dsp[:, 2:3], scalar=-FAR, in1=dsp[:, 0:1], op0=ALU.mult,
                                       op1=ALU.add).then_inc(s_i1, 1)
                dve.wait_ge(s_i1, i + 1)
                v.tensor_scalar(out=idx_tab[:, bass.ds(i, 1)].bitcast(I32), in0=tmp1, scalar1=FAR, scalar2=None,
                                op0=ALU.add).then_inc(s_idx, 1)

            def select(out, i, done):
                e = item_expert(dve, i)
                v.tensor_scalar(out=out, in0=ones, scalar1=sel_c[:, bass.ds(e, 1)], scalar2=None,
                                op0=ALU.mult).then_inc(done, 1)

            def splits(q, m):
                for r in range(PR - 1):
                    split(q, m * PR + r)

            def take_rows(i):
                dve.wait_ge(s_hh, i + 1)
                tt(hTl, turn_ps[:, :], hTh, ALU.subtract).then_inc(s_hl, 1)

            def take_act(i):
                dve.wait_ge(s_ah, i + 1)
                tt(aTl, turn_ps[:, :], aTh, ALU.subtract).then_inc(s_al, 1)

            def gate(i):
                dve.wait_ge(s_gf, i + 1)
                v.tensor_scalar(out=gb, in0=gate_ps[:, :], scalar1=LIMIT, scalar2=None, op0=ALU.min).then_inc(s_gb, 1)

            def activation(i):
                dve.wait_ge(s_uf, i + 1)
                v.tensor_scalar(out=ub, in0=up_ps[:, :], scalar1=LIMIT, scalar2=-LIMIT, op0=ALU.min,
                                op1=ALU.max).then_inc(s_u1, 1)
                dve.wait_ge(s_u1, i + 1)
                dve.wait_ge(s_gb, i + 1)
                v.scalar_tensor_tensor(out=ub, in0=ub, scalar=1.0, in1=gb, op0=ALU.add, op1=ALU.mult).then_inc(s_u2, 1)
                dve.wait_ge(s_u2, i + 1)
                dve.wait_ge(s_sg, i + 1)
                tt(ub, ub, sg).then_inc(s_acted, 1)

            def result(i):
                dve.wait_ge(s_df, i + 1)
                dve.wait_ge(s_landed, i + 1)
                v.tensor_scalar(out=yrow, in0=down_ps[:, :], scalar1=w_tab[:, bass.ds(i, 1)], scalar2=None,
                                op0=ALU.mult).then_inc(s_y, 1)

            rows_of(0)
            indices(0)
            rows_of(1)
            select(sel_gu, 0, s_selgu)
            split(0, 2)
            take_rows(0)
            indices(1)
            rows_of(2)
            splits(0, 1)
            gate(0)
            indices(2)

            def steps(q):
                splits(q, 5)
                if isinstance(q, int):
                    take_rows(1)
                    activation(0)
                select(sel_gu, q + 2, s_selgu)
                rows_of(q + 4)
                if not isinstance(q, int):
                    result(q)
                select(sel_d, q + 1, s_seld)
                splits(q, 6)
                gate(q + 2)
                take_act(q + 1)
                indices(q + 4)
                splits(q, 7)
                activation(q + 2)
                take_rows(q + 3)

            steps(-1)
            steady = steady_turns(dve)
            with dve.Fori(0, MAX_ITEMS // GROUP) as group:
                with dve.If(group * GROUP < steady):
                    with dve.Fori(0, GROUP) as n:
                        q = group * GROUP + n
                        with dve.If(q < steady):
                            steps(q)
            split(steady, FIRST + 12)
            split(steady, FIRST + 13)
            result(steady)
            take_act(steady + 1)
            for r in range(2, PR):
                split(steady, FIRST + 12 + r)
            select(sel_d, steady + 1, s_seld)
            result(steady + 1)

        @block.tensor
        def _(pe):
            T = nc.tensor

            def begin(u):
                turn, b = where[u]
                if turn:
                    pe.wait_ge(psum_free[b], turn)
                return bank[b]

            def end(ins, u):
                ins.then_inc(psum_full[where[u][1]], 1)

            def transposes(u, ins_):
                ps = begin(u)
                for n, a in enumerate(ins_):
                    k = a.shape[0]
                    last = T.transpose(ps[:, n * P:n * P + k], a, ident[0:k, 0:k])
                end(last, u)

            pe.wait_ge(s_const, 16)
            pe.wait_ge(s_par, 16 * 5)
            transposes("par", [praw[0:NPAR, :]])
            for t in range(NT):
                pe.wait_ge(s_xn, t + 1)
                for h in range(2):
                    transposes(f"xT{t}{'ab'[h]}", [xn[:, t % 2, k * P:(k + 1) * P] for k in range(4 * h, 4 * h + 4)])
            for t in range(NT):
                wait_taken(pe, f"xT{t}b")
            pe.wait_ge(s_win[0], 16)
            ps = begin("dt")
            for t in range(NT):
                for k in range(KT):
                    last = T.matmul(ps[:, t * 16:(t + 1) * 16], hTm[:, k, t * P:(t + 1) * P], w_in[:, k, DT0:INW],
                                    start=(k == 0), stop=(k == KT - 1))
            end(last, "dt")
            for ch in CHANNELS:
                ps = begin(f"xb{ch}")
                for k in range(KT):
                    last = T.matmul(ps[:, :], w_in[:, k, XBC0 + ch * P:XBC0 + (ch + 1) * P], hTm[:, k, :],
                                    start=(k == 0), stop=(k == KT - 1))
                end(last, f"xb{ch}")

            def project(u, t, a, b, src=None, w=None):
                src, w = (hTm, w_in) if src is None else (src, w)
                ps = begin(u)
                for k in range(KT):
                    last = T.matmul(ps[:, 0:b - a], src[:, k, t * P:(t + 1) * P], w[:, k, a:b],
                                    start=(k == 0), stop=(k == KT - 1))
                end(last, u)

            def heads(t):
                pe.wait_ge(s_rot, t + 1)
                transposes(f"tq{t}", [qk3[:, n * P:(n + 1) * P] for n in range(4)])
                transposes(f"tk{t}", [kd[:, n, :, :].rearrange("p a b -> p (a b)") for n in range(NKV)])

            k_seg = [0]

            def decays(c):
                if c == NT:
                    return
                ps = begin(f"cb{c}")
                for g in range(SG):
                    last = T.matmul(ps[:, g * P:(g + 1) * P], xc[:, 4 + g, c * P:(c + 1) * P],
                                    xc[:, 6 + g, c * P:(c + 1) * P], start=True, stop=True)
                end(last, f"cb{c}")
                for di, upto in (("f", c_le), ("b", c_ge)):
                    for g in range(SG):
                        u, k = f"sg{c}{di}{g}", k_seg[0]
                        pe.wait_ge(s_sm, k + 1)
                        ps = begin(u)
                        for h in range(HPG):
                            last = T.matmul(ps[:, h * P:(h + 1) * P], sm[k % 2][:, h, :], upto, start=True, stop=True)
                        end(last, u)
                        k_seg[0] += 1

            pe.wait_ge(s_win[1], 16)
            for t in (0, 1):
                project(f"q{t}", t, 0, AW)
                project(f"kv{t}", t, AW, Z0)
            pe.wait_ge(s_da, 1)
            for c in range(NT):
                ps = begin(f"cs{c}")
                f, b = da[:, c, 0:SH], da[:, c, SH:2 * SH]
                for n, (m, r) in enumerate(((c_le, f), (c_ge, b), (c_gt, f), (c_lt, b))):
                    T.matmul(ps[:, n * 8:n * 8 + 8], m, r, start=True, stop=True)
                end(T.matmul(ps[:, 32:48], ones, da[:, c, :], start=True, stop=True), f"cs{c}")
            heads(0)
            pe.wait_ge(s_xc, CT)
            for c in range(NT):
                transposes(f"tx{c}", [xc[:, n, c * P:(c + 1) * P] for n in range(4)])
                transposes(f"tb{c}", [xc[:, 4 + n, c * P:(c + 1) * P] for n in range(SG)])
            project("q2", 2, 0, AW)
            project("kv2", 2, AW, Z0)
            heads(1)
            project("q3", 3, 0, AW)
            project("kv3", 3, AW, Z0)
            pe.wait_ge(s_win[2], 16)
            project("z0", 0, Z0, XBC0)
            heads(2)
            decays(0)
            project("z1", 1, Z0, XBC0)
            project("z2", 2, Z0, XBC0)
            project("z3", 3, Z0, XBC0)
            heads(3)
            for c in range(NT):
                decays(c + 1)
                wait_taken(pe, f"tb{c}")
                pe.wait_ge(s_xdt, c + 1)
                pe.wait_ge(s_g, 4 * c + 4)
                ps = begin(f"yd{c}")
                xdtf, xdtb, xwf, xwb = xd[c % 2]
                for h in range(SH):
                    g, hh = divmod(h, HPG)
                    o = slice(h * HD, (h + 1) * HD)
                    T.matmul(ps[:, o], gdec[c % 2][g][:, hh, :], xdtf[:, o], start=True, stop=False)
                    last = T.matmul(ps[:, o], gdec[c % 2][2 + g][:, hh, :], xdtb[:, o], start=False, stop=True)
                end(last, f"yd{c}")
                for name, w, has in (("sf", xwf, c < NT - 1), ("sb", xwb, c > 0)):
                    if has:
                        ps = begin(f"{name}{c}")
                        for g in range(SG):
                            last = T.matmul(ps[:, g * GW:(g + 1) * GW], brows[:, c, g * SN:(g + 1) * SN],
                                            w[:, g * GW:(g + 1) * GW], start=True, stop=True)
                        end(last, f"{name}{c}")

            def attend(p):
                i, j = divmod(p, 4)
                if i and j == 0:
                    pe.wait_ge(s_ofree, i)
                for h in range(2):
                    wait_taken(pe, f"p{p}{'ab'[h]}")
                for h in range(2):
                    head = 2 * j + h
                    kv = head // (NH // NKV)
                    for kt in range(NT):
                        last = T.matmul(bank[7][:, head * HD:(head + 1) * HD], probsT[p % 2 * 2 + h][:, kt, :],
                                        vs[:, kt, kv * HD:(kv + 1) * HD], start=(kt == 0), stop=(kt == NT - 1))
                last.then_inc(s_of, 1)

            for t in range(NT):
                wait_taken(pe, f"tk{t}")
            for s in range(STEPS):
                if s < NPAIR:
                    i, j = divmod(s, 4)
                    pss = [begin(f"s{s}{h}") for h in "ab"]
                    for h in range(2):
                        r = slice(h * HD, (h + 1) * HD)
                        end(T.matmul(pss[h][:, :], qT[r, j, i * P:(i + 1) * P], kT[r, 2 * j // (NH // NKV), :],
                                     start=True, stop=True), f"s{s}{'ab'[h]}")
                if 1 <= s <= NPAIR:
                    for h in range(2):
                        wait_taken(pe, f"s{s - 1}{'ab'[h]}")
                        transposes(f"p{s - 1}{'ab'[h]}",
                                   [probs[(s - 1) % 2 * 2 + h][:, n * P:(n + 1) * P] for n in range(NT)])
                if 2 <= s <= NPAIR + 1:
                    attend(s - 2)
                if turn_at(s, 3) is not None:
                    c = turn_at(s, 3)
                    pe.wait_ge(s_prev, 1)
                    for name, prev, has in (("yf", prevf, c > 0), ("yb", prevb, c < NT - 1)):
                        if has:
                            ps = begin(f"{name}{c}")
                            for g in range(SG):
                                last = T.matmul(ps[:, g * GW:(g + 1) * GW], xc[:, 6 + g, c * P:(c + 1) * P],
                                                prev[c][:, g * GW:(g + 1) * GW], start=True, stop=True)
                            end(last, f"{name}{c}")
                if turn_at(s, TM) is not None:
                    t = turn_at(s, TM)
                    pe.wait_ge(s_mixa, t + 1)
                    transposes(f"tm{t}a", [mixa[:, n * P:(n + 1) * P] for n in range(4)])
                    pe.wait_ge(s_mixs, t + 1)
                    transposes(f"tm{t}b", [mixs[:, n * P:(n + 1) * P] for n in range(4)])
                if turn_at(s, OP) is not None:
                    t = turn_at(s, OP)
                    wait_taken(pe, f"tm{t}a")
                    wait_taken(pe, f"tm{t}b")
                    pe.wait_ge(s_wout, 16)
                    for h in range(2):
                        project(f"op{t}{'ab'[h]}", t, h * 512, h * 512 + 512, hTm, w_out)
                if turn_at(s, TH) is not None:
                    t = turn_at(s, TH)
                    pe.wait_ge(s_h, t + 1)
                    for h in range(2):
                        transposes(f"th{t}{'ab'[h]}", [hrw[:, k * P:(k + 1) * P] for k in range(4 * h, 4 * h + 4)])
                if turn_at(s, LG) is not None:
                    t = turn_at(s, LG)
                    wait_taken(pe, f"th{t}a")
                    wait_taken(pe, f"th{t}b")
                    pe.wait_ge(s_wr, 16)
                    ps = begin(f"lg{t}")
                    for k in range(KT):
                        last = T.matmul(ps[:, 0:NE], hrT[:, k, :], wr[:, k, :], start=(k == 0), stop=(k == KT - 1))
                    end(last, f"lg{t}")
            pe.wait_ge(s_cnt, 1)
            ps = begin("cum")
            every = msk.rearrange("p a b -> p (a b)")
            T.matmul(ps[:, 0:NT * NE], c_lt, every, start=True, stop=True)
            end(T.matmul(ps[:, NT * NE:2 * NT * NE], ones, every, start=True, stop=True), "cum")
            pe.wait_ge(s_tabr, 1)
            ps = begin("tab")
            end(T.matmul(ps[:, 0:3 * IW], ones, rhs3.rearrange("p a b -> p (a b)"), start=True, stop=True), "tab")

            for b in range(RINGB):
                turns = sum(1 for _, bb in where.values() if bb == b)
                pe.wait_ge(psum_free[b], turns)
            pe.wait_ge(s_ofree, NT)
            pe.wait_ge(s_tab, 1)

            def dispatch(i):
                pe.wait_ge(s_oh, i + 1)
                at_least(pe, s_dt, i)
                e = item_expert(pe, i)
                for t in range(NT):
                    last = T.matmul(down_ps[:, 0:3], onehot[:, t, :],
                                    payload[:, t, bass.ds(e, 1), :].rearrange("p a b -> p (a b)"),
                                    start=(t == 0), stop=(t == NT - 1))
                last.then_inc(s_dsp, 1)

            def turn_over(rows_, done):
                for k in range(KT):
                    last = T.transpose(turn_ps[:, k * P:(k + 1) * P], rows_[:, k * P:(k + 1) * P], ident)
                last.then_inc(done, 1)

            def turn_rows(i):
                pe.wait_ge(s_gath, 16 * i + 16)
                turn_over(hrow, s_hf)

            def turn_act(i):
                pe.wait_ge(s_acted, i + 1)
                pe.wait_ge(s_hl, i + 2)
                turn_over(ub, s_af)

            def product(q, m, kind, ps, xh, xl, sel, done):
                xh, xl = cut(xh, KT, P), cut(xl, KT, P)
                for r in range(PR):
                    pe.wait_ge(s_lo[r], turn(q, m * PR))
                    for kk in range(PK):
                        k = r * PK + kk
                        for n, (x, w) in enumerate(((xh, hi), (xh, lo), (xl, hi))):
                            for h in range(2):
                                last = T.matmul(ps[:, h * 512:h * 512 + 512], x[:, k, :],
                                                w[r][:, kk, h * 512:h * 512 + 512],
                                                start=(k == 0 and n == 0), stop=False)
                    last.then_inc(s_used[r], 1)
                selected, count = sel
                pe.wait_ge(selected[1], count)
                for h in range(2):
                    at_ = kind * DM + h * 512
                    last = T.matmul(ps[:, h * 512:h * 512 + 512], selected[0], btab[:, at_:at_ + 512],
                                    start=False, stop=True)
                last.then_inc(done, 1)

            def gate(q, m, i):
                pe.wait_ge(s_hl, i + 1)
                at_least(pe, s_gb, i)
                product(q, m, 0, gate_ps, hTh, hTl, ((sel_gu, s_selgu), i + 1), s_gf)

            def up(q, m, i):
                at_least(pe, s_u1, i)
                product(q, m, 1, up_ps, hTh, hTl, ((sel_gu, s_selgu), i + 1), s_uf)

            def down(q, m, i):
                pe.wait_ge(s_al, i + 1)
                at_least(pe, s_y, i)
                product(q, m, 2, down_ps, aTh, aTl, ((sel_d, s_seld), i + 1), s_df)

            pe.wait_ge(s_pay, 9)
            dispatch(0)
            dispatch(1)
            turn_rows(0)
            pe.wait_ge(s_btab, 1)
            gate(0, 0, 0)
            dispatch(2)
            up(0, 1, 0)
            turn_rows(1)

            def steps(q):
                gate(q, 5, q + 2)
                turn_act(q + 1)
                at_least(pe, s_y, q + 1)
                dispatch(q + 4)
                up(q, 6, q + 2)
                pe.wait_ge(s_al, q + 2)
                turn_rows(q + 3)
                pe.wait_ge(s_dt, q + 5)
                down(q, 7, q + 1)

            steps(-1)
            steady = steady_turns(pe)
            with pe.Fori(0, MAX_ITEMS // GROUP) as group:
                with pe.If(group * GROUP < steady):
                    with pe.Fori(0, GROUP) as n:
                        q = group * GROUP + n
                        with pe.If(q < steady):
                            steps(q)
            turn_act(steady + 1)
            down(steady, 5, steady + 1)


INPUTS = ["x", "norm_mix", "w_in", "q_norm", "k_norm", "conv_w", "conv_b", "dt_bias", "a_log", "d_skip",
          "ssm_norm", "attn_norm", "w_out", "norm_ffn", "w_router", "b_router", "w_gate", "b_gate",
          "w_up", "b_up", "w_down", "b_down"]


def kernel(**inputs):
    import concourse.bacc as bacc
    from concourse.bass_utils import run_bass_kernel_spmd

    nc = bacc.Bacc("TRN2", target_bir_lowering=False, num_devices=1)
    arrays, d = {}, {}
    for name in INPUTS:
        arrays[f"in_{name}"] = np.ascontiguousarray(inputs[name])
    arrays["in_const"] = constants()
    for name, a in arrays.items():
        d[name[3:]] = nc.dram_tensor(name, a.shape, mybir.dt.from_np(a.dtype), kind="ExternalInput").ap()
    out = nc.dram_tensor("out", (1, SEQ, DM), F32, kind="ExternalOutput").ap()
    hn = nc.dram_tensor("normed_rows", (SEQ, DM), F32, kind="Internal").ap()
    hybrid_layer(nc, d, out, hn)
    r = run_bass_kernel_spmd(nc, [arrays], core_ids=[0])
    return r.results[0]["out"]
```
